# Optimizing a Trainium2 kernel written in Bass

```python
import math
import jax, jax.numpy as jnp
from jax import lax
import numpy as np

D_MODEL = 1024
BATCH = 1
SEQ = 1024
DEPTH = 1

CHUNK = 64
GDN_HEADS = 4
GDN_DK = 128
GDN_DV = 128
GDN_QK = GDN_HEADS * GDN_DK
GDN_VW = GDN_HEADS * GDN_DV
CONV_K = 4
FX_HEADS = 8
FX_DH = 64
FX_W = FX_HEADS * FX_DH
Q_BLOCK = 128
PEER_HEADS = 8
PEER_NKEYS = 128
PEER_DKEY = 256
PEER_TOPK = 16
PEER_NEXPERTS = PEER_NKEYS * PEER_NKEYS
PEER_TOKEN_BLOCK = 128
DEEPNORM_ALPHA = (2.0 * DEPTH) ** 0.25
DEEPNORM_BETA = (8.0 * DEPTH) ** -0.25
IN_SIZES = (GDN_QK, GDN_QK, GDN_VW, GDN_VW, GDN_HEADS, GDN_HEADS, FX_W, FX_W, FX_W, FX_HEADS, D_MODEL, D_MODEL)
IN_WIDTH = sum(IN_SIZES)
IN_VALUE_SEGMENTS = (2, 8)

kernel_name = 'hybrid_gdn_fox_peer_deepnorm'

def _layernorm(x, g, b, eps=1e-5):
    xf = x.astype(jnp.float32)
    mu = jnp.mean(xf, axis=-1, keepdims=True)
    var = jnp.mean(jnp.square(xf - mu), axis=-1, keepdims=True)
    y = (xf - mu) * lax.rsqrt(var + eps) * g.astype(jnp.float32) + b.astype(jnp.float32)
    return y.astype(x.dtype)

def _l2norm(x, eps=1e-6):
    return x * lax.rsqrt(jnp.sum(jnp.square(x), axis=-1, keepdims=True) + eps)

def _causal_depthwise_conv(x, w):
    kw, c = w.shape
    return lax.conv_general_dilated(x, w[:, None, :].astype(x.dtype), window_strides=(1,), padding=[(kw - 1, 0)], dimension_numbers=('NWC', 'WIO', 'NWC'), feature_group_count=c)

def _gated_delta_rule(q, k, v, g, beta):
    b, h, s, dk = q.shape
    dv = v.shape[-1]
    n = s // CHUNK
    q = q.reshape(b, h, n, CHUNK, dk)
    k = k.reshape(b, h, n, CHUNK, dk)
    v = v.reshape(b, h, n, CHUNK, dv)
    g = g.reshape(b, h, n, CHUNK)
    beta = beta.reshape(b, h, n, CHUNK)
    gc = jnp.cumsum(g, axis=-1)
    tril = jnp.tril(jnp.ones((CHUNK, CHUNK), bool))
    strict = jnp.tril(jnp.ones((CHUNK, CHUNK), bool), -1)
    diff = gc[..., :, None] - gc[..., None, :]
    decay = jnp.where(tril, jnp.exp(jnp.where(tril, diff, 0.0)), 0.0)
    kb = k * beta[..., None]
    m = jnp.where(strict, jnp.einsum('bhnid,bhnjd->bhnij', kb, k) * decay, 0.0)
    a = m + jnp.eye(CHUNK, dtype=m.dtype)
    rhs = jnp.concatenate([v * beta[..., None], kb * jnp.exp(gc)[..., None]], axis=-1)
    sol = lax.linalg.triangular_solve(a, rhs, left_side=True, lower=True)
    u, w = sol[..., :dv], sol[..., dv:]
    qk = jnp.einsum('bhnid,bhnjd->bhnij', q, k) * decay
    qg = q * jnp.exp(gc)[..., None]
    glast = gc[..., -1]
    kd = k * jnp.exp(glast[..., None] - gc)[..., None]

    def step(state, inp):
        u_n, w_n, qk_n, qg_n, kd_n, gl_n = inp
        v_new = u_n - jnp.einsum('bhcd,bhde->bhce', w_n, state)
        o = jnp.einsum('bhcd,bhde->bhce', qg_n, state) + jnp.einsum('bhij,bhje->bhie', qk_n, v_new)
        state = state * jnp.exp(gl_n)[..., None, None] + jnp.einsum('bhcd,bhce->bhde', kd_n, v_new)
        return state, o

    xs = (jnp.moveaxis(u, 2, 0), jnp.moveaxis(w, 2, 0), jnp.moveaxis(qk, 2, 0), jnp.moveaxis(qg, 2, 0), jnp.moveaxis(kd, 2, 0), jnp.moveaxis(glast, 2, 0))
    s0 = jnp.zeros((b, h, dk, dv), jnp.float32)
    _, o = lax.scan(step, s0, xs)
    return jnp.moveaxis(o, 0, 2).reshape(b, h, s, dv)

def _gdn_branch(gq, gk, gv, gz, ga, gb, conv_w, a_log, dt_bias, norm_w, w_out):
    f32 = jnp.float32
    b, s, _ = gq.shape
    qkv = jax.nn.silu(_causal_depthwise_conv(jnp.concatenate([gq, gk, gv], axis=-1), conv_w))
    q, k, v = jnp.split(qkv, [GDN_QK, 2 * GDN_QK], axis=-1)
    q = _l2norm(q.reshape(b, s, GDN_HEADS, GDN_DK).transpose(0, 2, 1, 3).astype(f32)) * (GDN_DK ** -0.5)
    k = _l2norm(k.reshape(b, s, GDN_HEADS, GDN_DK).transpose(0, 2, 1, 3).astype(f32))
    v = v.reshape(b, s, GDN_HEADS, GDN_DV).transpose(0, 2, 1, 3).astype(f32)
    g = -jnp.exp(a_log.astype(f32)) * jax.nn.softplus(ga.astype(f32) + dt_bias.astype(f32))
    beta = jax.nn.sigmoid(gb.astype(f32))
    o = _gated_delta_rule(q, k, v, g.transpose(0, 2, 1), beta.transpose(0, 2, 1))
    o = o.transpose(0, 2, 1, 3)
    o = o * lax.rsqrt(jnp.mean(jnp.square(o), axis=-1, keepdims=True) + 1e-6) * norm_w.astype(f32)
    z = gz.reshape(b, s, GDN_HEADS, GDN_DV).astype(f32)
    o = (o * jax.nn.silu(z)).reshape(b, s, GDN_VW).astype(gq.dtype)
    return o @ w_out

def _forgetting_attention(q, k, v, log_f):
    s_len = q.shape[1]
    scale = FX_DH ** -0.5
    c = jnp.cumsum(log_f, axis=1).transpose(0, 2, 1)
    outs = []
    for i in range(s_len // Q_BLOCK):
        lo, hi = i * Q_BLOCK, (i + 1) * Q_BLOCK
        sc = jnp.einsum('bqhd,bkhd->bhqk', q[:, lo:hi], k[:, :hi]).astype(jnp.float32) * scale
        sc = sc + c[:, :, lo:hi, None] - c[:, :, None, :hi]
        causal = (lo + jnp.arange(Q_BLOCK))[:, None] >= jnp.arange(hi)[None, :]
        sc = jnp.where(causal, sc, -1e30)
        p = jax.nn.softmax(sc, axis=-1)
        outs.append(jnp.einsum('bhqk,bkhd->bqhd', p.astype(v.dtype), v[:, :hi]))
    return jnp.concatenate(outs, axis=1)

def _fox_branch(fq, fk, fv, ff, f_bias, w_out):
    b, s, _ = fq.shape
    q = fq.reshape(b, s, FX_HEADS, FX_DH)
    k = fk.reshape(b, s, FX_HEADS, FX_DH)
    v = fv.reshape(b, s, FX_HEADS, FX_DH)
    log_f = jax.nn.log_sigmoid(ff.astype(jnp.float32) + f_bias.astype(jnp.float32))
    o = _forgetting_attention(q, k, v, log_f).reshape(b, s, FX_W)
    return o @ w_out

def _peer(h, wq, keys, u_tab, v_tab):
    b, s, d = h.shape
    t = b * s
    hf = h.reshape(t, d)
    q = (hf @ wq).reshape(t, PEER_HEADS, 2, PEER_DKEY // 2)
    scores = jnp.einsum('thpd,hpnd->thpn', q, keys).astype(jnp.float32)
    top_s, top_i = lax.top_k(scores, PEER_TOPK)
    cand = top_s[:, :, 0, :, None] + top_s[:, :, 1, None, :]
    cand_idx = top_i[:, :, 0, :, None] * PEER_NKEYS + top_i[:, :, 1, None, :]
    best_s, best_pos = lax.top_k(cand.reshape(t, PEER_HEADS, PEER_TOPK * PEER_TOPK), PEER_TOPK)
    expert = jnp.take_along_axis(cand_idx.reshape(t, PEER_HEADS, PEER_TOPK * PEER_TOPK), best_pos, axis=-1)
    gate = jax.nn.softmax(best_s, axis=-1).astype(h.dtype)
    nb = t // PEER_TOKEN_BLOCK
    hk = PEER_HEADS * PEER_TOPK
    expert = expert.reshape(nb, PEER_TOKEN_BLOCK, hk)
    gate = gate.reshape(nb, PEER_TOKEN_BLOCK, hk)
    hb = hf.reshape(nb, PEER_TOKEN_BLOCK, d)

    def block(args):
        h_blk, e_blk, g_blk = args
        u = jnp.take(u_tab, e_blk, axis=0)
        act = jax.nn.gelu(jnp.einsum('td,tkd->tk', h_blk, u), approximate=False) * g_blk
        vv = jnp.take(v_tab, e_blk, axis=0)
        return jnp.einsum('tk,tkd->td', act, vv)

    y = lax.map(block, (hb, expert, gate))
    return y.reshape(b, s, d)

def _layer(h, w_in, gdn_conv_w, gdn_a_log, gdn_dt_bias, gdn_norm_w, fox_f_bias, w_out_gdn, w_out_fox, w_o, ln1_g, ln1_b, peer_wq, peer_keys, peer_u, peer_v, ln2_g, ln2_b):
    proj = h @ w_in
    splits = np.cumsum(IN_SIZES)[:-1].tolist()
    gq, gk, gv, gz, ga, gb, fq, fk, fv, ff, gate_a, gate_b = jnp.split(proj, splits, axis=-1)
    y_a = _gdn_branch(gq, gk, gv, gz, ga, gb, gdn_conv_w, gdn_a_log, gdn_dt_bias, gdn_norm_w, w_out_gdn)
    y_b = _fox_branch(fq, fk, fv, ff, fox_f_bias, w_out_fox)
    mix = jax.nn.sigmoid(gate_a) * y_a + jax.nn.sigmoid(gate_b) * y_b
    h = _layernorm(DEEPNORM_ALPHA * h + mix @ w_o, ln1_g, ln1_b)
    h = _layernorm(DEEPNORM_ALPHA * h + _peer(h, peer_wq, peer_keys, peer_u, peer_v), ln2_g, ln2_b)
    return h

def setup_inputs(seed: int = 0) -> dict:
    key = jax.random.key(seed)
    ks = jax.random.split(key, 20)
    f32 = jnp.float32
    L = DEPTH
    beta = DEEPNORM_BETA
    col_scale = np.ones((IN_WIDTH,), np.float32)
    off = np.cumsum((0,) + IN_SIZES)
    for seg in IN_VALUE_SEGMENTS:
        col_scale[off[seg]:off[seg + 1]] = beta
    nrm = jax.random.normal
    x = nrm(ks[0], (BATCH, SEQ, D_MODEL), f32)
    w_in = nrm(ks[1], (L, D_MODEL, IN_WIDTH), f32) * (D_MODEL ** -0.5) * jnp.asarray(col_scale)
    gdn_conv_w = nrm(ks[2], (L, CONV_K, 2 * GDN_QK + GDN_VW), f32) * (CONV_K ** -0.5)
    gdn_a_log = jnp.log(jax.random.uniform(ks[3], (L, GDN_HEADS), f32, 1.0, 16.0))
    dt = jnp.exp(jax.random.uniform(ks[4], (L, GDN_HEADS), f32, math.log(1e-3), math.log(1e-1)))
    gdn_dt_bias = dt + jnp.log(-jnp.expm1(-dt))
    gdn_norm_w = 1.0 + 0.02 * nrm(ks[5], (L, GDN_DV), f32)
    fox_f_bias = 2.0 + 0.1 * nrm(ks[6], (L, FX_HEADS), f32)
    w_out_gdn = nrm(ks[7], (L, GDN_VW, D_MODEL), f32) * (GDN_VW ** -0.5) * beta
    w_out_fox = nrm(ks[8], (L, FX_W, D_MODEL), f32) * (FX_W ** -0.5) * beta
    w_o = nrm(ks[9], (L, D_MODEL, D_MODEL), f32) * (D_MODEL ** -0.5) * beta
    ln1_g = 1.0 + 0.02 * nrm(ks[10], (L, D_MODEL), f32)
    ln1_b = 0.02 * nrm(ks[11], (L, D_MODEL), f32)
    peer_wq = nrm(ks[12], (L, D_MODEL, PEER_HEADS * PEER_DKEY), f32) * (D_MODEL ** -0.5)
    peer_keys = nrm(ks[13], (L, PEER_HEADS, 2, PEER_NKEYS, PEER_DKEY // 2), f32) * ((PEER_DKEY // 2) ** -0.5)
    peer_u = nrm(ks[14], (L, PEER_NEXPERTS, D_MODEL), f32) * (D_MODEL ** -0.5)
    peer_v = nrm(ks[15], (L, PEER_NEXPERTS, D_MODEL), f32) * beta
    ln2_g = 1.0 + 0.02 * nrm(ks[16], (L, D_MODEL), f32)
    ln2_b = 0.02 * nrm(ks[17], (L, D_MODEL), f32)
    return {'x': x, 'w_in': w_in, 'gdn_conv_w': gdn_conv_w, 'gdn_a_log': gdn_a_log, 'gdn_dt_bias': gdn_dt_bias, 'gdn_norm_w': gdn_norm_w, 'fox_f_bias': fox_f_bias, 'w_out_gdn': w_out_gdn, 'w_out_fox': w_out_fox, 'w_o': w_o, 'ln1_g': ln1_g, 'ln1_b': ln1_b, 'peer_wq': peer_wq, 'peer_keys': peer_keys, 'peer_u': peer_u, 'peer_v': peer_v, 'ln2_g': ln2_g, 'ln2_b': ln2_b}

def reference(x, w_in, gdn_conv_w, gdn_a_log, gdn_dt_bias, gdn_norm_w, fox_f_bias, w_out_gdn, w_out_fox, w_o, ln1_g, ln1_b, peer_wq, peer_keys, peer_u, peer_v, ln2_g, ln2_b):
    h = x
    for l in range(DEPTH):
        h = _layer(h, w_in[l], gdn_conv_w[l], gdn_a_log[l], gdn_dt_bias[l], gdn_norm_w[l], fox_f_bias[l], w_out_gdn[l], w_out_fox[l], w_o[l], ln1_g[l], ln1_b[l], peer_wq[l], peer_keys[l], peer_u[l], peer_v[l], ln2_g[l], ln2_b[l])
    return h


_drawn_inputs = setup_inputs


def setup_inputs(seed=0):
    import zlib

    import numpy as np

    out = dict(_drawn_inputs(seed))
    spreads = {}
    factors = {'gdn_norm_w': 4.391, 'fox_f_bias': 35.928, 'ln2_g': 8.16, 'ln2_b': 8.214}
    for name, (base, spread) in spreads.items():
        noise = np.random.default_rng([zlib.crc32(name.encode()), seed]).standard_normal(out[name].shape)
        drawn = base * np.exp(spread * noise) if base else spread * noise
        out[name] = __import__('jax').numpy.asarray(drawn.astype(out[name].dtype))
    for name, factor in factors.items():
        out[name] = (out[name] * factor).astype(out[name].dtype)
    return out
```

```python
import concourse.bass as bass
from concourse import mybir
from contextlib import ExitStack

F32 = mybir.dt.float32
U32 = mybir.dt.uint32
ALU = mybir.AluOpType
ACT = mybir.ActivationFunctionType
AX = mybir.AxisListType

D = 1024
SEQ = 1024
P = 128
KB = D // P
T = 512
HALVES = SEQ // T
TT = T // P
GH = 4
FH = 8
FD = 64
PH = 8
TOPK = 16
ALPHA = 2.0 ** 0.25
NEG = -3.0e38
ROWS = 96
BETA0, FOX0 = 32, 64
LEVELS = 6
RING = 16
QUAD = 4

I_QKV, I_Z, I_SM, I_FQK, I_FV, I_MIX, I_WO, I_PQ = 0, 12, 13, 14, 22, 23, 31, 33
ITEMS = 49


def build(nc, x, xT, w_qkv, w_z, w_sm, w_fqk, w_fv, w_mix, w_out, w_pq, conv_w, bias96, alog96,
          norm_w, ln, experts, out):
    ctx = ExitStack()
    with ctx:
        def sb(name, shape, dt=F32):
            return ctx.enter_context(nc.sbuf_tensor(name, shape, dt))

        def sem(name):
            return ctx.enter_context(nc.semaphore(name))

        def sems(name, n=2):
            return [sem(f"{name}{i}") for i in range(n)]

        B = [ctx.enter_context(nc.psum_tensor(f"bank{i}", [P, 512], F32)) for i in range(8)]
        d_rows = nc.dram_tensor("d_rows", [ROWS, SEQ], F32, kind="Internal").ap()
        d_fqk = nc.dram_tensor("d_fqk", [8, P, SEQ], F32, kind="Internal").ap()
        d_fv = nc.dram_tensor("d_fv", [SEQ, 512], F32, kind="Internal").ap()

        ident = sb("ident", [P, P])
        ones = sb("ones", [P, P])
        incl = sb("incl", [P, P])
        strict = sb("strict", [P, P])
        levmask = sb("levmask", [P, LEVELS + 1, P])
        negup = sb("negup", [P, P])
        state = sb("state", [P, GH, P])
        halo = sb("halo", [P, 12, 3])
        cw = sb("cw", [P, 12, 4])
        bias_c = sb("bias_c", [ROWS, 1])
        alog_c = sb("alog_c", [ROWS, 1])
        fcarry = sb("fcarry", [P, 1])
        eps_l2 = sb("eps_l2", [P, 1])
        normB = sb("normB", [P, P])
        ln2B = sb("ln2B", [P, 2, D])
        wslot = sb("wslot", [P, 2, 4096])
        h1 = sb("h1", [P, TT, D])
        eidx = sb("eidx", [P, TT, PH, TOPK], U32)
        gate = sb("gate", [P, TT, PH, TOPK])
        iota16 = sb("iota16", [P, TOPK])

        arena = sb("arena", [P, RING * 2 * D])

        class Region:
            def __init__(self, at):
                self.at = at

            def take(self, *shape, rows=P):
                n = 1
                for s in shape:
                    n *= s
                v = arena[0:rows, self.at:self.at + n]
                self.at += n
                assert self.at <= RING * 2 * D, self.at
                if len(shape) == 2:
                    v = v.rearrange("p (a b) -> p a b", a=shape[0])
                if len(shape) == 3:
                    v = v.rearrange("p (a b c) -> p a b c", a=shape[0], b=shape[1])
                return v

        base = Region(0)
        xTs = base.take(KB, T)
        oTg = base.take(GH, T)
        a1 = Region(base.at)
        qkvT = a1.take(12, T)
        zs = a1.take(TT, 512)
        rowsT = a1.take(TT, ROWS)
        a2 = Region(a1.at)
        raw = a2.take(2, T + 3)
        acc = a2.take(2, T)
        cwc = a2.take(2, 4)
        sm = [a2.take(T, rows=ROWS) for _ in range(6)]
        rows = a2.take(T, rows=ROWS)
        onesr = a2.take(T, rows=ROWS)
        a3 = Region(a1.at)
        gB, bB = a3.take(GH, P), a3.take(GH, P)
        sq = a3.take(8, P)
        nr = a3.take(8, P)
        qn, kn, kbT, qg, egB, DT, DTs, vt, kbg, kd, vb, MT, QK, X, Tm, Pm, wT, u, vn = (
            a3.take(GH, P) for _ in range(19))
        MS = a3.take(2, GH * P)
        o, og = DTs, kbT
        osq = vt
        colS = a3.take(ROWS)
        gd, egc, be, ss, rs4 = (a3.take(GH) for _ in range(5))
        b1 = Region(base.at)
        Osb = b1.take(TT, 512)
        oTf = b1.take(4, T)
        fst = b1.take(2, T)
        fvs = b1.take(TT, 512)
        qh = b1.take(2, T, rows=FD)
        kh = b1.take(2, SEQ, rows=FD)
        vh = b1.take(2, SEQ // P, FD)
        cB = b1.take(2, SEQ)
        cBd = b1.take(TT, P)
        sx = b1.take(2, SEQ)
        pT = b1.take(SEQ // P, P)
        nm, rsum, rinv = b1.take(2), b1.take(2), b1.take(2)
        mixT = b1.take(KB, T)
        m1 = Region(base.at + 4096)
        m1.at = base.at + TT * 512 + 4 * T
        sg = m1.take(2, 2, T)
        mt = m1.take(2, T)
        h1T = m1.take(KB, T)
        xn = Region(0).take(TT, D)
        st = m1.take(2, 6)
        mv = m1.take(2)
        t1 = m1
        qp = t1.take(2, T)
        sc = t1.take(2, TT, P)
        tv = t1.take(2, TT, TOPK)
        ti = t1.take(2, TT, TOPK)
        tf = t1.take(2, TT, TOPK)
        assert t1.at <= b1.at - KB * T, (t1.at, b1.at)
        c1 = Region(base.at)
        cand = c1.take(TT, 256)
        bv = c1.take(TT, TOPK)
        bi = c1.take(TT, TOPK)
        ba, bb = c1.take(TT, TOPK), c1.take(TT, TOPK)
        fa, fb = c1.take(TT, TOPK), c1.take(TT, TOPK)
        eq = c1.take(TT * TOPK, TOPK)
        gsum = c1.take(TT)
        assert c1.at <= base.at + TT * 512 + 4 * T
        ln1B = Region(RING * 2 * D - 2 * D).take(2, D)
        assert max(a3.at, b1.at) <= RING * 2 * D - 2 * D
        ring = Region(0).take(RING, 2 * D)

        s_const, s_load, s_cst2 = sem("s_const"), sem("s_load"), sem("s_cst2")
        s_xT, s_xn, s_ln1 = sem("s_xT"), sem("s_xn"), sem("s_ln1")
        s_w = sems("s_w")
        s_wdone = sem("s_wdone")
        s_raw, s_conv, s_silu = sems("s_raw"), sems("s_conv"), sems("s_silu")
        s_nat, s_natev = sem("s_nat"), sems("s_natev")
        s_smE, s_smU, s_smL, s_smX = sem("s_smE"), sem("s_smU"), sem("s_smL"), sem("s_smX")
        s_rows, s_rowst, s_rT, s_rTe = sem("s_rows"), sem("s_rowst"), sem("s_rT"), sem("s_rTe")
        s_gb = sem("s_gb")
        g = {k: sem("g_" + k) for k in (
            "sq", "ssum", "norm", "qk", "diff", "exps", "decay", "prod", "mt", "scaled", "kbg", "x0", "t0p",
            "t0", "ms", "lp", "lpe", "lt", "lx", "wu", "wte", "ue", "ws", "vn", "o", "S",
            "osq", "ss", "rt", "og", "ogt", "oT")}
        s_fev, s_fst, s_fvst = sems("s_fev"), sems("s_fst"), sem("s_fvst")
        s_att, s_attd = sems("s_att"), sems("s_attd")
        s_S, s_sc, s_ex = sems("s_S"), sems("s_sc"), sems("s_ex")
        s_T, s_Te, s_O, s_Oe = sem("s_T"), sem("s_Te"), sem("s_O"), sems("s_Oe")
        s_OT, s_OTe = sem("s_OT"), sem("s_OTe")
        s_sg, s_mix = sems("s_sg"), sems("s_mix")
        s_hp, s_var, s_std, s_h1 = sem("s_hp"), sem("s_var"), sem("s_std"), sem("s_h1")
        s_hT, s_hTe = sem("s_hT"), sem("s_hTe")
        s_pq, s_pqe, s_scr, s_sce, s_top = sems("s_pq"), sems("s_pqe"), sems("s_scr"), sems("s_sce"), sems("s_top")
        s_gx, s_gxe, s_sel = sem("s_gx"), sem("s_gxe"), sem("s_sel")

        pm = sb("pm", [P, 2 * D + 4 * TOPK])
        h_cur = pm[:, 0:D]
        Y = pm[:, D:2 * D]
        diag = wslot[:, 0, 0:8 * P].rearrange("p (a b) -> p a b", a=8)
        dots = pm[:, 2 * D:2 * D + TOPK]
        gel = pm[:, 2 * D + TOPK:2 * D + 2 * TOPK]
        gcur = pm[:, 2 * D + 2 * TOPK:2 * D + 3 * TOPK]
        wgt = pm[:, 2 * D + 3 * TOPK:2 * D + 4 * TOPK]
        istage, icur, izero, ispare = (
            sb(n, [P, w], U32) for n, w in (("istage", TOPK), ("icur", TOPK), ("izero", QUAD), ("ispare", QUAD)))
        pst = sb("pst", [P, 2, 6])
        pmv = sb("pmv", [P, 2])
        s_idx, s_stage, s_gat, s_dot, s_gel, s_wgt, s_diag, s_pv, s_yadd = (
            sem("s_idx"), sem("s_stage"), sems("s_gat", 4), sem("s_dot"), sem("s_gel"), sem("s_wgt"), sem("s_diag"),
            sems("s_pv", 4), sem("s_yadd"))
        s_yv, s_ys, s_y, s_out = sem("s_yv"), sem("s_ys"), sem("s_y"), sem("s_out")

        block = ctx.enter_context(nc.Block())


        def item(n, w):
            return wslot[:, n % 2, 0:w * 128].rearrange("p (k c) -> p k c", k=w)

        def wide(n):
            return wslot[:, n % 2, :].rearrange("p (k c) -> p k c", k=KB)

        @block.sync
        def _(sp):
            for dst, src, s in ((cw[:, :, :], conv_w, s_fst[0]), (bias_c[:, :], bias96, s_fst[1]),
                                (alog_c[:, :], alog96, s_out), (normB[:, :], norm_w.to_broadcast([P, P]), s_load)):
                sp.dma_start(dst, src).then_inc(s, 16)
            for k in range(2):
                sp.dma_start(ln2B[:, k, :], ln[2 + k:3 + k, :].to_broadcast([P, D])).then_inc(s_load, 16)

            def load(n, dst, src, i=0):
                if n >= 2:
                    sp.wait_ge(s_wdone, n - 1 + 2 * i)
                sp.dma_start(dst, src).then_inc(s_w[n % 2], 16)

            for hf in range(HALVES):
                n0 = ITEMS * hf
                if hf:
                    sp.wait_ge(s_pv[3], 1 + TT * PH * hf)
                    sp.wait_ge(s_y, TT * hf)
                sp.dma_start(xTs, xT[:, hf * T:(hf + 1) * T].rearrange("(k p) t -> p k t", p=P)).then_inc(s_xT, 16)
                for k in range(2):
                    sp.dma_start(ln1B[:, k, :], ln[k:k + 1, :].to_broadcast([P, D])).then_inc(s_ln1, 16)
                for j in range(2):
                    load(n0 + j, item(n0 + j, 8), w_qkv[j])
                with sp.Fori(0, 5) as i:
                    for j in range(2):
                        n = n0 + 2 + j
                        load(n, item(n, 8), w_qkv[bass.ds(2 * i + 2 + j, 1)].rearrange("a p k c -> p (a k) c"), i)
                load(n0 + I_Z, wide(n0 + I_Z), w_z)
                n = n0 + I_SM
                load(n, wslot[:, n % 2, 0:KB * ROWS].rearrange("p (k c) -> p k c", k=KB), w_sm)
                for j in range(2):
                    n = n0 + I_FQK + j
                    load(n, item(n, 8), w_fqk[j])
                sp.wait_ge(s_rows, hf + 1)
                sp.dma_start(d_rows[:, hf * T:(hf + 1) * T], rows).then_inc(s_rowst, 16)
                sp.wait_ge(s_rowst, 16 * (hf + 1))
                sp.wait_ge(s_rTe, hf + 1)
                with sp.Fori(0, TT) as c:
                    sp.wait_ge(g["decay"], 1 + c + TT * hf)
                    for dst, r in ((gB, 0), (bB, BETA0)):
                        for h in range(GH):
                            sp.dma_start(dst[:, h, :], d_rows[r + h:r + h + 1, bass.ds(c * P + hf * T, P)]
                                         .to_broadcast([P, P])).then_inc(s_gb, 16)
                with sp.Fori(0, 3) as i:
                    for j in range(2):
                        n = n0 + I_FQK + 2 + j
                        load(n, item(n, 8), w_fqk[bass.ds(2 * i + 2 + j, 1)].rearrange("a p k c -> p (a k) c"), i)
                load(n0 + I_FV, wide(n0 + I_FV), w_fv)
                for j in range(2):
                    n = n0 + I_MIX + j
                    load(n, item(n, 24), w_mix[j])
                W = T * (hf + 1)
                for j in range(2):
                    sp.wait_ge(s_fst[j], 16 + 16 * 4 * (hf + 1))
                sp.wait_ge(s_fvst, 16 * (hf + 1))
                with sp.Fori(0, FH // 2) as i:
                    for j in range(2):
                        sp.wait_ge(s_attd[j], 1 + i + 4 * hf)
                        sp.dma_start(qh[:, j, :], d_fqk[bass.ds(2 * i, 1), FD * j:FD * (j + 1), hf * T:(hf + 1) * T]
                                     .rearrange("a p t -> p (a t)")).then_inc(s_att[j], 16)
                        sp.dma_start(kh[:, j, 0:W], d_fqk[bass.ds(2 * i + 1, 1), FD * j:FD * (j + 1), 0:W]
                                     .rearrange("a p t -> p (a t)")).then_inc(s_att[j], 16)
                        sp.dma_start(vh[:, j, 0:W // P, :], d_fv[0:W, bass.ds(i * P + FD * j, FD)]
                                     .rearrange("(k p) d -> p k d", p=P)).then_inc(s_att[j], 16)
                        sp.dma_start(cB[:, j, 0:W], d_rows[bass.ds(2 * i + (FOX0 + j), 1), 0:W]
                                     .to_broadcast([P, W])).then_inc(s_att[j], 16)
                with sp.Fori(0, 3) as i:
                    for j in range(2):
                        n = n0 + I_MIX + 2 + j
                        load(n, item(n, 24), w_mix[bass.ds(2 * i + 2 + j, 1)].rearrange("a p k c -> p (a k) c"), i)
                for j in range(2):
                    load(n0 + I_WO + j, wide(n0 + I_WO + j), w_out[j])
                sp.wait_ge(s_wdone, n0 + I_WO)
                sp.dma_start(xn, x[hf * T:(hf + 1) * T, :].rearrange("(t p) d -> p t d", p=P)).then_inc(s_xn, 16)
                with sp.Fori(0, PH) as i:
                    for j in range(2):
                        n = n0 + I_PQ + j
                        load(n, item(n, 9), w_pq[bass.ds(2 * i + j, 1)].rearrange("a p k c -> p (a k) c"), i)
                with sp.Fori(0, TT) as t:
                    sp.wait_ge(s_y, t + (TT * hf + 1))
                    sp.dma_start(out[bass.ds(t * P + hf * T, P), :], Y).then_inc(s_out, 16)
            sp.wait_ge(s_out, 16 + 16 * TT * HALVES)

        @block.gpsimd
        def _(pool):
            for s in (*s_fev, *s_raw, *s_conv, *s_silu, *s_attd, *s_sc, s_T, s_O, s_Te, *s_Oe, *s_mix, *s_pqe, *s_sce,
                      *s_top, *s_pv, s_yadd, g["decay"], g["lp"], g["S"]):
                pool.sem_inc(s, 1)
            pool.memset(ones[:, :], 1.0)
            pool.memset(ident[:, :], 0.0)
            pool.memset(state[:, :, :], 0.0)
            pool.memset(halo[:, :, :], 0.0)
            pool.memset(fcarry[:, :], 0.0)
            pool.memset(eps_l2[:, :], 1e-6)
            pool.memset(negup[:, :], 1e30)
            pool.iota(iota16[:, :], [[1, TOPK]], base=0, channel_multiplier=0, allow_small_or_imprecise_dtypes=True)
            pool.drain()
            pool.affine_select(out=ident[:, :], in_=ident[:, :], compare_op=ALU.not_equal, fill=1.0, base=0,
                               pattern=[[-1, P]], channel_multiplier=1)
            pool.affine_select(out=incl[:, :], in_=ones[:, :], compare_op=ALU.is_ge, fill=0.0, base=0,
                               pattern=[[1, P]], channel_multiplier=-1)
            pool.affine_select(out=strict[:, :], in_=ones[:, :], compare_op=ALU.is_gt, fill=0.0, base=0,
                               pattern=[[1, P]], channel_multiplier=-1)
            pool.affine_select(out=negup[:, :], in_=negup[:, :], compare_op=ALU.is_gt, fill=0.0, base=0,
                               pattern=[[1, P]], channel_multiplier=-1)
            for l in range(LEVELS + 1):
                s = 1 << l
                nb = P // (2 * s)
                v = levmask[:, l, :].rearrange("p (b h r) -> p b h r", b=nb, h=2)
                pool.memset(v[:, :, 0, :], 0.0)
                w = v[:, :, 1, :]
                pool.drain()
                pool.affine_select(out=w, in_=ones[:, 0:nb * s].rearrange("p (b r) -> p b r", b=nb),
                                   compare_op=ALU.is_ge, fill=0.0, base=0,
                                   pattern=[[-2 * s, nb], [0, s]], channel_multiplier=1)
                pool.drain()
                pool.affine_select(out=w, in_=w, compare_op=ALU.is_gt, fill=0.0, base=s,
                                   pattern=[[2 * s, nb], [0, s]], channel_multiplier=-1)
            pool.drain()
            pool.memset(izero[:, :], 0).then_inc(s_const, 1)
            for hf in range(HALVES):
                with pool.Fori(0, TT) as c:
                    pool.wait_ge(g["mt"], c + (TT * hf + 1))
                    for l in range(LEVELS):
                        if l >= 2:
                            pool.wait_ge(g["lp"], 1 + c * LEVELS + (TT * hf * LEVELS + l - 1))
                        else:
                            pool.wait_ge(g["lp"], 1 + c * LEVELS + TT * hf * LEVELS)
                        for h in range(GH):
                            last = pool.tensor_tensor(MS[:, l % 2, h * P:(h + 1) * P], MT[:, h, :],
                                                      levmask[:, l + 1, :], ALU.mult)
                        last.then_inc(g["ms"], 1)
                pool.wait_ge(s_sel, PH * (hf + 1))
                pool.wait_ge(s_h1, TT * (hf + 1))
                with pool.Fori(0, TT) as t:
                    with pool.Fori(0, PH) as h:
                        b = t * PH + h
                        pool.tensor_copy(istage[:, :], eidx[:, bass.ds(t, 1), bass.ds(h, 1), :]
                                         .rearrange("p a b k -> p (a b k)")).then_inc(s_stage, 1)
                        pool.wait_ge(s_stage, b + (TT * PH * hf + 1))
                        for q in range(4):
                            pool.wait_ge(s_pv[q], 1 + b + TT * PH * hf)
                            pool.tensor_tensor(icur[:, 4 * q:4 * q + 4], istage[:, 4 * q:4 * q + 4], izero[:, :],
                                               ALU.add).then_inc(s_idx, 1)
                            pool.wait_ge(s_idx, 8 * b + (8 * TT * PH * hf + 2 * q + 1))
                            pool.tensor_tensor(ispare[:, :], izero[:, :], izero[:, :], ALU.add).then_inc(s_idx, 1)
                            for k in range(QUAD * q, QUAD * q + QUAD):
                                pool.indirect_dma_start(
                                    out=ring[:, k, :], out_offset=None, in_=experts,
                                    in_offset=bass.IndirectOffsetOnAxis(ap=icur[:, k:k + 1], axis=0),
                                ).then_inc(s_gat[q], 16)

        @block.scalar
        def _(act):
            act.wait_ge(s_const, 1)
            act.wait_ge(s_load, 16 * 3)
            act.wait_ge(s_fst[0], 16)
            act.wait_ge(s_fst[1], 16)
            act.wait_ge(s_out, 16)

            act.activation(alog_c[:, :], alog_c[:, :], ACT.Exp).then_inc(s_cst2, 1)
            for hf in range(HALVES):
                n0 = ITEMS * hf
                if hf:
                    act.wait_ge(s_y, TT * hf)
                with act.Fori(0, 6) as i:
                    for j in range(2):
                        act.wait_ge(s_wdone, 2 * i + (n0 + j + 1))
                        act.wait_ge(s_conv[j], 1 + i + 6 * hf)
                        act.activation(raw[:, j, 3:T + 3], B[j][:, :], ACT.Copy).then_inc(s_raw[j], 1)
                        act.wait_ge(s_conv[j], 1 + i + (6 * hf + 1))
                        act.activation(qkvT[:, bass.ds(2 * i + j, 1), :].rearrange("p a t -> p (a t)"),
                                       acc[:, j, :], ACT.Silu).then_inc(s_silu[j], 1)
                for tt in range(TT):
                    act.wait_ge(s_nat, 16 * hf + tt + 1)
                    act.activation(zs[:, tt, :], B[2 + tt % 2][:, :], ACT.Silu).then_inc(s_natev[tt % 2], 1)
                act.wait_ge(s_smE, hf + 1)
                act.activation(sm[2], sm[1], ACT.Exp, scale=-1.0)
                act.activation(sm[5], sm[0], ACT.Exp, scale=-1.0).then_inc(s_smX, 1)
                act.wait_ge(s_smU, hf + 1)
                act.activation(sm[4], sm[3], ACT.Ln).then_inc(s_smL, 1)
                act.wait_ge(s_rT, hf + 1)
                act.activation(rowsT[:, :, :], B[5][:, 0:TT * ROWS].rearrange("p (a b) -> p a b", a=TT),
                               ACT.Copy).then_inc(s_rTe, 1)
                with act.Fori(0, TT) as c:
                    tau = c + (TT * hf + 1)
                    act.wait_ge(g["ssum"], tau)
                    for k in range(2):
                        act.activation(nr[:, 4 * k:4 * k + 4, :].rearrange("p a b -> p (a b)"), B[k][:, :],
                                       ACT.Sqrt, bias=eps_l2[:, :]).then_inc(g["norm"], 1)
                    act.wait_ge(g["diff"], tau)
                    act.activation(egB, gB, ACT.Exp)
                    act.activation(DT, DT, ACT.Exp)
                    act.activation(gd, gd, ACT.Exp)
                    act.activation(egc, colS[:, 0:GH], ACT.Exp)
                    act.activation(vt, qkvT[:, 8:12, bass.ds(c * P, P)], ACT.Copy).then_inc(g["exps"], 1)
                    act.wait_ge(g["prod"], tau)
                    for h in range(GH):
                        act.activation(kd[:, h, :], B[2][:, h * P:(h + 1) * P], ACT.Copy, scale=gd[:, h:h + 1])
                        last = act.activation(vb[:, h, :], B[3][:, h * P:(h + 1) * P], ACT.Copy,
                                              scale=colS[:, BETA0 + h:BETA0 + h + 1])
                    last.then_inc(g["scaled"], 1)
                    act.wait_ge(g["t0p"], tau)
                    act.activation(Tm.rearrange("p a b -> p (a b)"), B[6][:, :], ACT.Copy).then_inc(g["t0"], 1)
                    for l in range(LEVELS):
                        act.wait_ge(g["lp"], 1 + c * LEVELS + (TT * hf * LEVELS + l + 1))
                        act.activation(Pm.rearrange("p a b -> p (a b)"), B[7][:, :], ACT.Copy).then_inc(g["lpe"], 1)
                    act.wait_ge(g["wu"], tau)
                    act.activation(wT.rearrange("p a b -> p (a b)"), B[1][:, :], ACT.Copy).then_inc(g["wte"], 1)
                    act.wait_ge(g["o"], tau)
                    act.activation(o.rearrange("p a b -> p (a b)"), B[4][:, :], ACT.Copy)
                    act.drain()
                    act.activation(osq, o, ACT.Square).then_inc(g["osq"], 1)
                    act.wait_ge(g["ss"], tau)
                    act.activation(rs4, ss, ACT.Sqrt).then_inc(g["rt"], 1)
                    act.wait_ge(g["ogt"], tau)
                    act.activation(oTg[:, :, bass.ds(c * P, P)],
                                   B[6][:, :].rearrange("p (a b) -> p a b", a=GH), ACT.Copy).then_inc(g["oT"], 1)
                with act.Fori(0, 4) as i:
                    for j in range(2):
                        act.wait_ge(s_wdone, 2 * i + (n0 + I_FQK + j + 1))
                        act.wait_ge(s_fst[j], 16 + 16 * i + 64 * hf)
                        act.activation(fst[:, j, :], B[j][:, :], ACT.Copy,
                                       scale=(FD ** -0.5 if j == 0 else 1.0)).then_inc(s_fev[j], 1)
                        act.wait_ge(s_fev[j], 1 + i + (4 * hf + 1))
                        act.dma_start(d_fqk[bass.ds(2 * i + j, 1), :, hf * T:(hf + 1) * T]
                                      .rearrange("a p t -> p (a t)"), fst[:, j, :]).then_inc(s_fst[j], 16)
                for tt in range(TT):
                    act.wait_ge(s_nat, 16 * hf + 4 + tt + 1)
                    act.activation(fvs[:, tt, :], B[2 + tt % 2][:, :], ACT.Copy).then_inc(s_natev[tt % 2], 1)
                for k in range(2):
                    act.wait_ge(s_natev[k], 8 * hf + 4)
                act.dma_start(d_fv[hf * T:(hf + 1) * T, :].rearrange("(t p) c -> p t c", p=P), fvs).then_inc(s_fvst, 16)
                with act.Fori(0, FH // 2) as i:
                    it = i + 4 * hf

                    def softmax(m):
                        nk = 4 * hf + m % 4 + 1
                        act.wait_ge(s_sc[m % 2], 1 + 4 * it + (m // 2 + 1))
                        act.activation(sx[:, m % 2, 0:nk * P], sx[:, m % 2, 0:nk * P], ACT.Exp,
                                       bias=nm[:, m % 2:m % 2 + 1],
                                       accum_out=rsum[:, m % 2:m % 2 + 1]).then_inc(s_ex[m % 2], 1)

                    softmax(0)
                    for m in range(8):
                        if m < 7:
                            softmax(m + 1)
                        nk = 4 * hf + m % 4 + 1
                        act.wait_ge(s_T, 1 + 8 * it + (m + 1))
                        act.wait_ge(s_O, 1 + 8 * it + m)
                        for k0 in range(0, nk, 4):
                            k1 = min(nk, k0 + 4)
                            last = act.activation(pT[:, k0:k1, :].rearrange("p a b -> p (a b)"),
                                                  B[4 + k0 // 4][:, 0:(k1 - k0) * P], ACT.Copy)
                        last.then_inc(s_Te, 1)
                for tt in range(TT):
                    act.wait_ge(s_OT, 4 * hf + tt + 1)
                    act.activation(oTf[:, :, tt * P:(tt + 1) * P],
                                   B[4 + tt % 2][:, :].rearrange("p (a b) -> p a b", a=4), ACT.Copy).then_inc(s_OTe, 1)
                with act.Fori(0, 4) as i:
                    for j in range(2):
                        act.wait_ge(s_wdone, 2 * i + (n0 + I_MIX + j + 1))
                        act.wait_ge(s_mix[j], 1 + i + 4 * hf)
                        for k in range(2):
                            last = act.activation(sg[:, j, k, :], B[4 * j + k][:, :], ACT.Sigmoid)
                        last.then_inc(s_sg[j], 1)
                for tt in range(TT):
                    act.wait_ge(s_var, 4 * hf + tt + 1)
                    act.activation(mv[:, 1:2], mv[:, 1:2], ACT.Sqrt).then_inc(s_std, 1)
                for tt in range(TT):
                    act.wait_ge(s_hT, 4 * hf + tt + 1)
                    for k in range(2):
                        last = act.activation(h1T[:, 4 * k:4 * k + 4, tt * P:(tt + 1) * P],
                                              B[2 * (tt % 2) + k][:, :].rearrange("p (a b) -> p a b", a=4), ACT.Copy)
                    last.then_inc(s_hTe, 1)
                with act.Fori(0, PH) as i:
                    for j in range(2):
                        act.wait_ge(s_pq[j], i + (PH * hf + 1))
                        act.activation(qp[:, j, :], B[j][:, :], ACT.Copy).then_inc(s_pqe[j], 1)
                    for j in range(2):
                        act.wait_ge(s_scr[j], i + (PH * hf + 1))
                        act.wait_ge(s_top[j], 1 + i + PH * hf)
                        act.activation(sc[:, j, :, :], B[2 + j][:, :].rearrange("p (a b) -> p a b", a=TT),
                                       ACT.Copy).then_inc(s_sce[j], 1)
                    act.wait_ge(s_gx, i + (PH * hf + 1))
                    act.activation(bv, bv, ACT.Exp).then_inc(s_gxe, 1)
                with act.Fori(0, TT) as t:
                    with act.Fori(0, PH) as h:
                        b4 = 4 * (t * PH + h) + 4 * TT * PH * hf

                        def gelu(q):
                            act.wait_ge(s_dot, b4 + (q + 1))
                            act.activation(gel[:, 4 * q:4 * q + 4], dots[:, 4 * q:4 * q + 4], ACT.Gelu).then_inc(s_gel, 1)

                        gelu(0)
                        for q in range(4):
                            if q < 3:
                                gelu(q + 1)
                            act.wait_ge(s_wgt, b4 + (q + 1))
                            if q >= 2:
                                act.wait_ge(s_pv[q - 2], 1 + t * PH + h + (TT * PH * hf + 1))
                            for k in range(4 * q, 4 * q + 4):
                                last = act.activation(diag[:, k % 8, :], ident[:, :], ACT.Copy, scale=wgt[:, k:k + 1])
                            last.then_inc(s_diag, 1)
                        act.wait_ge(s_pv[3], 1 + t * PH + h + (TT * PH * hf + 1))
                    act.wait_ge(s_yv, t + (TT * hf + 1))
                    act.activation(pmv[:, 1:2], pmv[:, 1:2], ACT.Sqrt).then_inc(s_ys, 1)

        @block.vector
        def _(dve):
            dve.wait_ge(s_const, 1)
            dve.wait_ge(s_load, 16 * 3)
            dve.wait_ge(s_fst[0], 16)
            dve.wait_ge(s_fst[1], 16)
            dve.wait_ge(s_out, 16)

            dve.wait_ge(s_cst2, 1)
            dve.tensor_scalar(alog_c[:, :], alog_c[:, :], -1.0, None, ALU.mult)
            dve.drain()

            def top16(vals, v16, i16):
                dve.max(v16[:, 0:8], vals)
                dve.drain()
                dve.max_index(i16[:, 0:8].bitcast(U32), v16[:, 0:8], vals)
                dve.drain()
                dve.match_replace(vals, v16[:, 0:8], vals, NEG)
                dve.drain()
                dve.max(v16[:, 8:16], vals)
                dve.drain()
                dve.max_index(i16[:, 8:16].bitcast(U32), v16[:, 8:16], vals)

            def layernorm(v, gb, stats, mean_var, s_v, v_val, s_s, s_val):
                for k in range(2):
                    dve.bn_stats(stats[:, k, :], v[:, k * 512:(k + 1) * 512])
                dve.drain()
                dve.bn_aggr(mean_var[:, 0:2], stats[:, :, :].rearrange("p a b -> p (a b)"))
                dve.drain()
                dve.tensor_scalar(mean_var[:, 1:2], mean_var[:, 1:2], 1e-5, None, ALU.add).then_inc(s_v, 1)
                dve.wait_ge(s_s, s_val)
                dve.reciprocal(mean_var[:, 1:2], mean_var[:, 1:2])
                dve.drain()
                dve.tensor_scalar(v, v, mean_var[:, 0:1], mean_var[:, 1:2], ALU.subtract, ALU.mult)
                dve.drain()
                dve.tensor_tensor(v, v, gb[:, 0, :], ALU.mult)
                dve.drain()
                return dve.tensor_tensor(v, v, gb[:, 1, :], ALU.add)

            for hf in range(HALVES):
                n0 = ITEMS * hf
                if hf:
                    dve.wait_ge(s_y, TT * hf)
                with dve.Fori(0, 6) as i:
                    for j in range(2):
                        rj, aj = raw[:, j, :], acc[:, j, :]
                        blk = bass.ds(2 * i + j, 1)
                        dve.wait_ge(s_silu[j], 1 + i + 6 * hf)
                        dve.tensor_copy(cwc[:, j, :], cw[:, blk, :].rearrange("p a k -> p (a k)"))
                        dve.tensor_copy(rj[:, 0:3], halo[:, blk, :].rearrange("p a k -> p (a k)"))
                        dve.drain()
                        dve.wait_ge(s_raw[j], 1 + i + (6 * hf + 1))
                        dve.tensor_scalar(aj, rj[:, 0:T], cwc[:, j, 0:1], None, ALU.mult)
                        for k in range(1, 4):
                            dve.drain()
                            last = dve.scalar_tensor_tensor(aj, rj[:, k:k + T], cwc[:, j, k:k + 1], aj,
                                                            ALU.mult, ALU.add)
                            if k == 1:
                                dve.tensor_copy(halo[:, blk, :].rearrange("p a k -> p (a k)"), rj[:, T:T + 3])
                        last.then_inc(s_conv[j], 1)
                dve.wait_ge(s_wdone, n0 + I_SM + 1)
                V, A, E, U, L, XS = sm
                dve.tensor_scalar(V, B[4][0:ROWS, :], bias_c[:, :], None, ALU.add)
                dve.memset(onesr, 1.0)
                dve.drain()
                dve.scalar_tensor_tensor(A, V, -1.0, V, ALU.mult, ALU.max).then_inc(s_smE, 1)
                dve.wait_ge(s_smX, hf + 1)
                dve.tensor_scalar(U, E, 1.0, None, ALU.add).then_inc(s_smU, 1)
                dve.drain()
                dve.tensor_scalar(A, U, -1.0, None, ALU.add)
                dve.drain()
                dve.tensor_scalar(rows, A, 0.0, None, ALU.is_equal)
                dve.tensor_scalar(A, A, 1e-30, None, ALU.max)
                dve.drain()
                dve.reciprocal(A, A)
                dve.tensor_tensor(rows, rows, E, ALU.mult)
                dve.drain()
                dve.tensor_tensor(A, A, E, ALU.mult)
                dve.drain()
                dve.wait_ge(s_smL, hf + 1)
                dve.tensor_tensor(L, L, A, ALU.mult)
                dve.drain()
                dve.tensor_tensor(L, L, rows, ALU.add)
                dve.tensor_scalar(A, V, 0.0, None, ALU.max)
                dve.tensor_scalar(U, V, 0.0, None, ALU.min)
                dve.tensor_scalar(XS, XS, 1.0, None, ALU.add)
                dve.drain()
                dve.tensor_tensor(A, A, L, ALU.add)
                dve.tensor_tensor(U, U, L, ALU.subtract)
                dve.reciprocal(rows, XS)
                dve.drain()
                dve.tensor_scalar(A, A, alog_c[:, :], None, ALU.mult)
                dve.drain()
                for tt in range(TT):
                    s = slice(tt * P, (tt + 1) * P)
                    dve.tensor_tensor_scan(rows[0:GH, s], onesr[0:GH, s], A[0:GH, s], 0.0, ALU.mult, ALU.add)
                dve.tensor_tensor_scan(rows[FOX0:FOX0 + FH, :], onesr[FOX0:FOX0 + FH, :], U[FOX0:FOX0 + FH, :],
                                       fcarry[FOX0:FOX0 + FH, :], ALU.mult, ALU.add).then_inc(s_rows, 1)
                dve.drain()
                dve.tensor_copy(fcarry[FOX0:FOX0 + FH, :], rows[FOX0:FOX0 + FH, T - 1:T])
                dve.wait_ge(s_rTe, hf + 1)
                dve.wait_ge(s_rowst, 16 * (hf + 1))
                with dve.Fori(0, TT) as c:
                    tau = c + (TT * hf + 1)
                    qk = qkvT[:, 0:8, bass.ds(c * P, P)]
                    dve.wait_ge(s_silu[0], 1 + 6 * (hf + 1))
                    dve.wait_ge(s_silu[1], 1 + 6 * (hf + 1))
                    dve.tensor_tensor(sq, qk, qk, ALU.mult).then_inc(g["sq"], 1)
                    dve.tensor_copy(colS, rowsT[:, bass.ds(c, 1), :].rearrange("p a b -> p (a b)"))
                    dve.drain()
                    dve.wait_ge(s_gb, 128 * c + 128 * (TT * hf + 1))
                    for h in range(GH):
                        dve.tensor_scalar(DT[:, h, :], gB[:, h, :], colS[:, h:h + 1], 0.0, ALU.subtract, ALU.min)
                    dve.tensor_tensor(gd, gB[:, :, P - 1], colS[:, 0:GH], ALU.subtract).then_inc(g["diff"], 1)
                    dve.wait_ge(g["norm"], 2 * c + 2 * (TT * hf + 1))
                    dve.reciprocal(nr, nr)
                    dve.drain()
                    dve.scalar_tensor_tensor(qn, qkvT[:, 0:4, bass.ds(c * P, P)], P ** -0.5, nr[:, 0:4, :],
                                             ALU.mult, ALU.mult)
                    dve.tensor_tensor(kn, qkvT[:, 4:8, bass.ds(c * P, P)], nr[:, 4:8, :], ALU.mult)
                    dve.drain()
                    dve.tensor_tensor(kbT, kn, bB, ALU.mult).then_inc(g["qk"], 1)
                    dve.wait_ge(g["exps"], tau)
                    dve.tensor_tensor(DT, DT, incl[:, None, :].to_broadcast([P, GH, P]), ALU.mult)
                    dve.tensor_tensor(qg, qn, egB, ALU.mult)
                    dve.tensor_tensor(be, egc, colS[:, BETA0:BETA0 + GH], ALU.mult)
                    dve.drain()
                    dve.tensor_tensor(DTs, DT, strict[:, None, :].to_broadcast([P, GH, P]), ALU.mult).then_inc(g["decay"], 1)
                    dve.drain()
                    dve.wait_ge(g["prod"], tau)
                    dve.tensor_tensor(MT.rearrange("p a b -> p (a b)"), B[4][:, :],
                                      DTs.rearrange("p a b -> p (a b)"), ALU.mult).then_inc(g["mt"], 1)
                    dve.drain()
                    dve.tensor_tensor(X, MT, levmask[:, 0:1, :].to_broadcast([P, GH, P]), ALU.mult)
                    dve.drain()
                    dve.tensor_tensor(X, ident[:, None, :].to_broadcast([P, GH, P]), X, ALU.subtract).then_inc(g["x0"], 1)
                    dve.tensor_tensor(QK.rearrange("p a b -> p (a b)"), B[5][:, :],
                                      DT.rearrange("p a b -> p (a b)"), ALU.mult)
                    dve.wait_ge(g["scaled"], tau)
                    for h in range(GH):
                        last = dve.tensor_scalar(kbg[:, h, :], B[2][:, h * P:(h + 1) * P], be[:, h:h + 1], None, ALU.mult)
                    last.then_inc(g["kbg"], 1)
                    dve.drain()
                    dve.wait_ge(g["t0"], tau)
                    for l in range(LEVELS):
                        if l:
                            dve.drain()
                        dve.wait_ge(g["lt"], c * LEVELS + (TT * hf * LEVELS + l + 1))
                        if l < LEVELS - 1:
                            dve.tensor_tensor(Tm.rearrange("p a b -> p (a b)"), Tm.rearrange("p a b -> p (a b)"),
                                              B[6][:, :], ALU.subtract)
                        dve.tensor_tensor(X.rearrange("p a b -> p (a b)"), X.rearrange("p a b -> p (a b)"),
                                          B[0][:, :], ALU.subtract).then_inc(g["lx"], 1)
                    dve.wait_ge(g["wu"], tau)
                    dve.tensor_copy(u.rearrange("p a b -> p (a b)"), B[2][:, :])
                    dve.drain()
                    dve.wait_ge(g["ws"], tau)
                    dve.tensor_tensor(vn.rearrange("p a b -> p (a b)"), u.rearrange("p a b -> p (a b)"),
                                      B[3][:, :], ALU.subtract).then_inc(g["vn"], 1)
                    dve.wait_ge(g["o"], tau)
                    for h in range(GH):
                        last = dve.scalar_tensor_tensor(state[:, h, :], state[:, h, :], egB[:, h, P - 1:P],
                                                        B[5][:, h * P:(h + 1) * P], ALU.mult, ALU.add)
                    last.then_inc(g["S"], 1)
                    dve.wait_ge(g["osq"], tau)
                    dve.tensor_reduce(ss, osq, AX.X, ALU.add)
                    dve.drain()
                    dve.tensor_scalar(ss, ss, 1.0 / P, 1e-6, ALU.mult, ALU.add).then_inc(g["ss"], 1)
                    dve.wait_ge(g["rt"], tau)
                    dve.reciprocal(rs4, rs4)
                    dve.drain()
                    for h in range(GH):
                        dve.scalar_tensor_tensor(og[:, h, :], o[:, h, :], rs4[:, h:h + 1], normB[:, :], ALU.mult, ALU.mult)
                    dve.drain()
                    for k in range(2):
                        dve.wait_ge(s_natev[k], 8 * hf + 2)
                    dve.tensor_tensor(og.rearrange("p a b -> p (a b)"), og.rearrange("p a b -> p (a b)"),
                                      zs[:, bass.ds(c, 1), :].rearrange("p a b -> p (a b)"), ALU.mult).then_inc(g["og"], 1)
                with dve.Fori(0, FH // 2) as i:
                    it = i + 4 * hf

                    def scores(m):
                        j, qt, r = m // 4, m % 4, m % 2
                        nk = 4 * hf + qt + 1
                        if qt == 0:
                            dve.wait_ge(s_att[j], 64 * it + 64)
                            dve.tensor_tensor(cBd, cB[:, j, hf * T:(hf + 1) * T].rearrange("p (a b) -> p a b", a=TT),
                                              negup[:, None, :].to_broadcast([P, TT, P]), ALU.add)
                            dve.drain()
                        dve.wait_ge(s_S[r], 4 * it + (m // 2 + 1))
                        dve.wait_ge(s_T, 8 * it + max(m, 1))
                        n_full = (nk - 1) * P
                        for k0 in range(0, n_full, 512):
                            k1 = min(n_full, k0 + 512)
                            dve.tensor_tensor(sx[:, r, k0:k1], B[2 * r + k0 // 512][:, 0:k1 - k0], cB[:, j, k0:k1],
                                              ALU.subtract)
                        off = n_full % 512
                        dve.tensor_tensor(sx[:, r, n_full:n_full + P], B[2 * r + n_full // 512][:, off:off + P],
                                          cBd[:, qt, :], ALU.subtract)
                        dve.drain()
                        dve.tensor_reduce(nm[:, r:r + 1], sx[:, r, 0:nk * P], AX.X, ALU.max, negate=True).then_inc(s_sc[r], 1)

                    scores(0)
                    for m in range(8):
                        if m < 7:
                            scores(m + 1)
                        j, qt, r = m // 4, m % 4, m % 2
                        dve.wait_ge(s_O, 1 + 8 * it + (m + 1))
                        dve.reciprocal(rinv[:, r:r + 1], rsum[:, r:r + 1])
                        dve.drain()
                        dve.tensor_scalar(Osb[:, qt, bass.ds(i * P + FD * j, FD)], B[6 + r][:, 0:FD], rinv[:, r:r + 1],
                                          None, ALU.mult).then_inc(s_Oe[r], 1)
                        if qt == 3:
                            dve.drain().then_inc(s_attd[j], 1)
                with dve.Fori(0, 4) as i:
                    for j in range(2):
                        dve.drain()
                        dve.wait_ge(s_sg[j], i + (4 * hf + 1))
                        for k in range(2):
                            dve.tensor_tensor(mt[:, k, :], sg[:, j, k, :], B[4 * j + 2 + k][:, :], ALU.mult)
                        dve.drain()
                        dve.tensor_tensor(mixT[:, bass.ds(2 * i + j, 1), :].rearrange("p a t -> p (a t)"),
                                          mt[:, 0, :], mt[:, 1, :], ALU.add).then_inc(s_mix[j], 1)
                dve.wait_ge(s_xn, 16 * (hf + 1))
                dve.wait_ge(s_ln1, 32 * (hf + 1))
                for nh in range(2):
                    for tt in range(TT):
                        dve.wait_ge(s_nat, 16 * hf + 8 + 4 * nh + tt + 1)
                        dve.scalar_tensor_tensor(h1[:, tt, nh * 512:(nh + 1) * 512], xn[:, tt, nh * 512:(nh + 1) * 512],
                                                 ALPHA, B[2 + tt % 2][:, :], ALU.mult, ALU.add).then_inc(s_natev[tt % 2], 1)
                dve.drain()
                for tt in range(TT):
                    layernorm(h1[:, tt, :], ln1B, st, mv, s_var, None, s_std, 4 * hf + tt + 1).then_inc(s_h1, 1)
                    dve.drain()
                with dve.Fori(0, PH) as i:
                    for j in range(2):
                        dve.wait_ge(s_sce[j], 1 + i + (PH * hf + 1))
                        dve.memset(tv[:, j, :, :], NEG)
                        dve.drain()
                        for tt in range(TT):
                            top16(sc[:, j, tt, :], tv[:, j, tt, :], ti[:, j, tt, :])
                        dve.drain()
                        dve.tensor_copy(tf[:, j, :, :], ti[:, j, :, :].bitcast(U32)).then_inc(s_top[j], 1)
                    dve.drain()
                    for tt in range(TT):
                        dve.tensor_tensor(cand[:, tt, :].rearrange("p (a b) -> p a b", a=TOPK),
                                          tv[:, 0, tt, :, None].to_broadcast([P, TOPK, TOPK]),
                                          tv[:, 1, tt, None, :].to_broadcast([P, TOPK, TOPK]), ALU.add)
                    dve.drain()
                    for tt in range(TT):
                        top16(cand[:, tt, :], bv[:, tt, :], bi[:, tt, :])
                    dve.drain()
                    dve.tensor_scalar(ba.bitcast(U32), bi.bitcast(U32), 4, None, ALU.logical_shift_right)
                    dve.tensor_scalar(bb.bitcast(U32), bi.bitcast(U32), 15, None, ALU.bitwise_and)
                    for tt in range(TT):
                        dve.tensor_scalar(gsum[:, tt:tt + 1], bv[:, tt, 0:1], 1.0, None, ALU.mult)
                    dve.drain()
                    for tt in range(TT):
                        last = dve.tensor_scalar(bv[:, tt, :], bv[:, tt, :], gsum[:, tt:tt + 1], None, ALU.subtract)
                    last.then_inc(s_gx, 1)
                    for src, f, k in ((ba, fa, 0), (bb, fb, 1)):
                        dve.tensor_copy(f, src.bitcast(U32))
                        dve.drain()
                        dve.tensor_tensor(eq, f.rearrange("p a b -> p (a b)")[:, :, None].to_broadcast([P, TT * TOPK, TOPK]),
                                          iota16[:, None, :].to_broadcast([P, TT * TOPK, TOPK]), ALU.is_equal)
                        dve.drain()
                        for tt in range(TT):
                            e = eq[:, tt * TOPK:(tt + 1) * TOPK, :]
                            dve.tensor_tensor(e, e, tf[:, k, tt, None, :].to_broadcast([P, TOPK, TOPK]), ALU.mult)
                        dve.drain()
                        dve.tensor_reduce(f.rearrange("p a b -> p (a b)"), eq, AX.X, ALU.add)
                        dve.drain()
                    dve.scalar_tensor_tensor(eidx[:, :, bass.ds(i, 1), :].rearrange("p t a k -> p t (a k)"),
                                             fa, float(P), fb, ALU.mult, ALU.add)
                    dve.wait_ge(s_gxe, i + (PH * hf + 1))
                    dve.tensor_reduce(gsum, bv, AX.X, ALU.add)
                    dve.drain()
                    dve.reciprocal(gsum, gsum)
                    dve.drain()
                    dve.tensor_tensor(gate[:, :, bass.ds(i, 1), :].rearrange("p t a k -> p t (a k)"), bv,
                                      gsum[:, :, None].to_broadcast([P, TT, TOPK]), ALU.mult).then_inc(s_sel, 1)
                    dve.drain()
                with dve.Fori(0, TT) as t:
                    if hf:
                        dve.wait_ge(s_out, 16 + 16 * t + 16 * TT * hf)
                    else:
                        dve.wait_ge(s_out, 16 + 16 * t)
                    dve.tensor_copy(h_cur, h1[:, bass.ds(t, 1), :].rearrange("p a d -> p (a d)"))
                    dve.drain()
                    dve.tensor_scalar(Y, h_cur, ALPHA, None, ALU.mult)
                    with dve.Fori(0, PH) as h:
                        b = t * PH + h
                        b4 = 4 * b + 4 * TT * PH * hf
                        dve.tensor_copy(gcur, gate[:, bass.ds(t, 1), bass.ds(h, 1), :].rearrange("p a b k -> p (a b k)"))

                        def weigh(q):
                            dve.wait_ge(s_gel, b4 + (q + 1))
                            dve.tensor_tensor(wgt[:, 4 * q:4 * q + 4], gel[:, 4 * q:4 * q + 4],
                                              gcur[:, 4 * q:4 * q + 4], ALU.mult).then_inc(s_wgt, 1)

                        for q in range(4):
                            dve.wait_ge(s_gat[q], 64 * b + 64 * (TT * PH * hf + 1))
                            for k in range(4 * q, 4 * q + 4):
                                last = dve.tensor_tensor_reduce(
                                    out=ring[:, k, 0:D], in0=ring[:, k, 0:D], in1=h_cur, scale=1.0, scalar=0.0,
                                    op0=ALU.mult, op1=ALU.add, accum_out=dots[:, k:k + 1])
                            last.then_inc(s_dot, 1)
                            if q == 0:
                                dve.drain()
                            if q:
                                weigh(q - 1)
                        weigh(3)
                        dve.wait_ge(s_pv[3], 1 + b + (TT * PH * hf + 1))
                        for k in range(2):
                            last = dve.tensor_tensor(Y[:, k * 512:(k + 1) * 512], Y[:, k * 512:(k + 1) * 512],
                                                     B[6 + k][:, :], ALU.add)
                        last.then_inc(s_yadd, 1)
                        dve.drain()
                    layernorm(Y, ln2B, pst, pmv, s_yv, None, s_ys, t + (TT * hf + 1)).then_inc(s_y, 1)

        @block.tensor
        def _(pe):
            pe.wait_ge(s_const, 1)

            def block_mm(bank, w, rhs, nk=KB, k0=0):
                for k in range(nk):
                    last = pe.matmul(bank[:, :], w[:, k0 + k, :], rhs[:, k, :], start=(k == 0), stop=(k == nk - 1))
                return last

            def natural(n, call, hf, lhs):
                pe.wait_ge(s_w[n % 2], 16 * (n // 2 + 1))
                w = wide(n)
                for tt in range(TT):
                    pe.wait_ge(s_natev[tt % 2], 8 * hf + 2 * call + tt // 2)
                    for k in range(KB):
                        last = pe.matmul(B[2 + tt % 2][:, :], lhs[:, k, tt * P:(tt + 1) * P], w[:, k, :],
                                         start=(k == 0), stop=(k == KB - 1))
                    last.then_inc(s_nat, 1)
                pe.drain().then_inc(s_wdone, 1)

            def transpose4(bank, src):
                for h in range(4):
                    last = pe.transpose(bank[:, h * P:(h + 1) * P], src[:, h, :], ident[:, :])
                return last

            def heads(bank, lhs, rhs):
                for h in range(GH):
                    last = pe.matmul(bank[:, h * P:(h + 1) * P], lhs[:, h, :], rhs[:, h, :], start=True, stop=True)
                return last

            for hf in range(HALVES):
                n0 = ITEMS * hf
                pe.wait_ge(s_xT, 16 * (hf + 1))
                with pe.Fori(0, 6) as i:
                    for j in range(2):
                        n = n0 + j
                        pe.wait_ge(s_w[n % 2], 16 * i + 16 * (n // 2 + 1))
                        pe.wait_ge(s_raw[j], 1 + i + 6 * hf)
                        block_mm(B[j], item(n, 8), xTs).then_inc(s_wdone, 1)
                natural(n0 + I_Z, 0, hf, xTs)
                n = n0 + I_SM
                pe.wait_ge(s_w[n % 2], 16 * (n // 2 + 1))
                w = wslot[:, n % 2, 0:KB * ROWS].rearrange("p (k c) -> p k c", k=KB)
                for k in range(KB):
                    last = pe.matmul(B[4][0:ROWS, :], w[:, k, :], xTs[:, k, :], start=(k == 0), stop=(k == KB - 1))
                last.then_inc(s_wdone, 1)
                pe.wait_ge(s_rows, hf + 1)
                for tt in range(TT):
                    last = pe.transpose(B[5][:, tt * ROWS:(tt + 1) * ROWS], rows[:, tt * P:(tt + 1) * P],
                                        ident[0:ROWS, 0:ROWS])
                last.then_inc(s_rT, 1)
                pe.wait_ge(s_raw[0], 1 + 6 * (hf + 1))
                pe.wait_ge(s_raw[1], 1 + 6 * (hf + 1))
                with pe.Fori(0, TT) as c:
                    tau = c + (TT * hf + 1)
                    lev = c * LEVELS
                    pe.wait_ge(g["sq"], tau)
                    for k in range(2):
                        last = pe.matmul(B[k][:, :], ones[:, :], sq[:, 4 * k:4 * k + 4, :].rearrange("p a b -> p (a b)"),
                                         start=True, stop=True)
                    last.then_inc(g["ssum"], 1)
                    pe.wait_ge(g["qk"], tau)
                    pe.wait_ge(g["exps"], tau)
                    transpose4(B[2], kn)
                    transpose4(B[3], vt)
                    heads(B[4], kn, kbT)
                    heads(B[5], kn, qn).then_inc(g["prod"], 1)
                    pe.wait_ge(g["x0"], tau)
                    transpose4(B[6], X).then_inc(g["t0p"], 1)
                    pe.wait_ge(g["t0"], tau)
                    for l in range(LEVELS):
                        pe.wait_ge(g["ms"], lev + (TT * hf * LEVELS + l + 1))
                        if l:
                            pe.wait_ge(g["lx"], lev + (TT * hf * LEVELS + l))
                        msl = MS[:, l % 2, :].rearrange("p (a b) -> p a b", a=GH)
                        heads(B[7], msl, Tm).then_inc(g["lp"], 1)
                        pe.wait_ge(g["lpe"], lev + (TT * hf * LEVELS + l + 1))
                        if l < LEVELS - 1:
                            heads(B[6], X, Pm)
                        heads(B[0], Pm, X).then_inc(g["lt"], 1)
                    pe.wait_ge(g["lx"], lev + (TT * hf * LEVELS + LEVELS))
                    pe.wait_ge(g["kbg"], tau)
                    heads(B[1], kbg, X)
                    heads(B[2], X, vb).then_inc(g["wu"], 1)
                    pe.wait_ge(g["wte"], tau)
                    pe.wait_ge(g["S"], 1 + c + TT * hf)
                    heads(B[3], wT, state).then_inc(g["ws"], 1)
                    pe.wait_ge(g["vn"], tau)
                    for h in range(GH):
                        s = slice(h * P, (h + 1) * P)
                        pe.matmul(B[4][:, s], qg[:, h, :], state[:, h, :], start=True, stop=False)
                        pe.matmul(B[4][:, s], QK[:, h, :], vn[:, h, :], start=False, stop=True)
                    heads(B[5], kd, vn).then_inc(g["o"], 1)
                    pe.wait_ge(g["og"], tau)
                    transpose4(B[6], og).then_inc(g["ogt"], 1)
                pe.wait_ge(g["oT"], TT * (hf + 1))
                with pe.Fori(0, 4) as i:
                    for j in range(2):
                        n = n0 + I_FQK + j
                        pe.wait_ge(s_w[n % 2], 16 * i + 16 * (n // 2 + 1))
                        pe.wait_ge(s_fev[j], 1 + i + 4 * hf)
                        block_mm(B[j], item(n, 8), xTs).then_inc(s_wdone, 1)
                natural(n0 + I_FV, 1, hf, xTs)
                for k in range(2):
                    pe.wait_ge(s_natev[k], 8 * hf + 4)
                    pe.wait_ge(s_fev[k], 1 + 4 * (hf + 1))
                with pe.Fori(0, FH // 2) as i:
                    it = i + 4 * hf

                    def qk_scores(m):
                        j, qt, r = m // 4, m % 4, m % 2
                        nk = 4 * hf + qt + 1
                        if qt == 0:
                            pe.wait_ge(s_att[j], 64 * it + 64)
                        pe.wait_ge(s_sc[r], 1 + 4 * it + m // 2)
                        for k0 in range(0, nk * P, 512):
                            k1 = min(nk * P, k0 + 512)
                            last = pe.matmul(B[2 * r + k0 // 512][:, 0:k1 - k0], qh[:, j, qt * P:(qt + 1) * P],
                                             kh[:, j, k0:k1], start=True, stop=True)
                        last.then_inc(s_S[r], 1)

                    qk_scores(0)
                    for m in range(8):
                        if m < 7:
                            qk_scores(m + 1)
                        j, qt, r = m // 4, m % 4, m % 2
                        nk = 4 * hf + qt + 1
                        pe.wait_ge(s_ex[r], 4 * it + (m // 2 + 1))
                        pe.wait_ge(s_Te, 1 + 8 * it + m)
                        for k in range(nk):
                            last = pe.transpose(B[4 + k // 4][:, (k % 4) * P:(k % 4 + 1) * P],
                                                sx[:, r, k * P:(k + 1) * P], ident[:, :])
                        last.then_inc(s_T, 1)
                        pe.wait_ge(s_Te, 1 + 8 * it + (m + 1))
                        pe.wait_ge(s_Oe[r], 1 + 4 * it + m // 2)
                        for k in range(nk):
                            last = pe.matmul(B[6 + r][:, 0:FD], pT[:, k, :], vh[:, j, k, :], start=(k == 0), stop=(k == nk - 1))
                        last.then_inc(s_O, 1)
                for k in range(2):
                    pe.wait_ge(s_Oe[k], 1 + 16 * (hf + 1))
                for tt in range(TT):
                    if tt >= 2:
                        pe.wait_ge(s_OTe, 4 * hf + tt - 1)
                    transpose4(B[4 + tt % 2], Osb[:, tt, :].rearrange("p (a b) -> p a b", a=4)).then_inc(s_OT, 1)
                pe.wait_ge(s_OTe, 4 * (hf + 1))
                with pe.Fori(0, 4) as i:
                    for j in range(2):
                        n = n0 + I_MIX + j
                        pe.wait_ge(s_w[n % 2], 16 * i + 16 * (n // 2 + 1))
                        pe.wait_ge(s_mix[j], 1 + i + 4 * hf)
                        w = item(n, 24)
                        block_mm(B[4 * j], w, xTs)
                        block_mm(B[4 * j + 1], w, xTs, k0=8)
                        block_mm(B[4 * j + 2], w, oTg, nk=4, k0=16)
                        block_mm(B[4 * j + 3], w, oTf, nk=4, k0=20).then_inc(s_wdone, 1)
                for j in range(2):
                    pe.wait_ge(s_mix[j], 1 + 4 * (hf + 1))
                for nh in range(2):
                    natural(n0 + I_WO + nh, 2 + nh, hf, mixT)
                for k in range(2):
                    pe.wait_ge(s_natev[k], 8 * (hf + 1))
                for tt in range(TT):
                    pe.wait_ge(s_h1, 4 * hf + tt + 1)
                    if tt >= 2:
                        pe.wait_ge(s_hTe, 4 * hf + tt - 1)
                    for k in range(2):
                        last = transpose4(B[2 * (tt % 2) + k],
                                          h1[:, tt, k * 512:(k + 1) * 512].rearrange("p (a b) -> p a b", a=4))
                    last.then_inc(s_hT, 1)
                pe.wait_ge(s_hTe, 4 * (hf + 1))
                with pe.Fori(0, PH) as i:
                    for j in range(2):
                        n = n0 + I_PQ + j
                        pe.wait_ge(s_w[n % 2], 16 * i + 16 * (n // 2 + 1))
                        pe.wait_ge(s_pqe[j], 1 + i + PH * hf)
                        block_mm(B[j], item(n, 9), h1T).then_inc(s_pq[j], 1)
                    for j in range(2):
                        n = n0 + I_PQ + j
                        pe.wait_ge(s_pqe[j], 1 + i + (PH * hf + 1))
                        pe.wait_ge(s_sce[j], 1 + i + PH * hf)
                        for tt in range(TT):
                            last = pe.matmul(B[2 + j][:, tt * P:(tt + 1) * P], qp[:, j, tt * P:(tt + 1) * P],
                                             item(n, 9)[:, 8, :], start=True, stop=True)
                        last.then_inc(s_scr[j], 1)
                    pe.drain().then_inc(s_wdone, 2)
                with pe.Fori(0, TT) as t:
                    with pe.Fori(0, PH) as h:
                        b = t * PH + h
                        b4 = 4 * b + 4 * TT * PH * hf
                        pe.wait_ge(s_yadd, 1 + b + TT * PH * hf)
                        for q in range(4):
                            pe.wait_ge(s_diag, b4 + (q + 1))
                            for k in range(4 * q, 4 * q + 4):
                                for n in range(2):
                                    last = pe.matmul(B[6 + n][:, :], diag[:, k % 8, :],
                                                     ring[:, k, D + n * 512:D + (n + 1) * 512],
                                                     start=(k == 0), stop=(k == TOPK - 1))
                            last.then_inc(s_pv[q], 1)


def kernel(x, w_in, gdn_conv_w, gdn_a_log, gdn_dt_bias, gdn_norm_w, fox_f_bias, w_out_gdn, w_out_fox,
           w_o, ln1_g, ln1_b, peer_wq, peer_keys, peer_u, peer_v, ln2_g, ln2_b):
    import numpy as np
    import concourse.bacc as bacc
    from concourse.bass_utils import run_bass_kernel_spmd

    def blocks(w, width):
        k, n = w.shape
        return np.ascontiguousarray(w.reshape(k // 128, 128, n // width, width).transpose(2, 1, 0, 3))

    w = np.asarray(w_in)[0]
    o = np.cumsum([0, 512, 512, 512, 512, 4, 4, 512, 512, 512, 8, 1024, 1024])
    small = np.zeros((1024, ROWS), np.float32)
    small[:, 0:4], small[:, BETA0:BETA0 + 4], small[:, FOX0:FOX0 + 8] = (
        w[:, o[4]:o[5]], w[:, o[5]:o[6]], w[:, o[9]:o[10]])
    fq, fk = blocks(w[:, o[6]:o[7]], 128), blocks(w[:, o[7]:o[8]], 128)
    bias = np.zeros((ROWS, 1), np.float32)
    bias[0:4, 0], bias[FOX0:FOX0 + 8, 0] = gdn_dt_bias[0], fox_f_bias[0]
    alog = np.zeros((ROWS, 1), np.float32)
    alog[0:4, 0] = gdn_a_log[0]
    keys = np.asarray(peer_keys)[0].reshape(16, 128, 128).transpose(0, 2, 1)[:, :, None, :]
    arrays = {
        "x": np.asarray(x)[0],
        "xT": np.ascontiguousarray(np.asarray(x)[0].T),
        "w_qkv": blocks(w[:, 0:o[3]], 128),
        "w_z": blocks(w[:, o[3]:o[4]], 512)[0],
        "w_sm": blocks(small, ROWS)[0],
        "w_fqk": np.ascontiguousarray(np.stack([fq, fk], 1).reshape(8, 128, 8, 128)),
        "w_fv": blocks(w[:, o[8]:o[9]], 512)[0],
        "w_mix": np.ascontiguousarray(np.concatenate(
            [blocks(w[:, o[10]:o[11]], 128), blocks(w[:, o[11]:o[12]], 128),
             blocks(np.asarray(w_out_gdn)[0], 128), blocks(np.asarray(w_out_fox)[0], 128)], 2)),
        "w_out": blocks(np.asarray(w_o)[0], 512),
        "w_pq": np.ascontiguousarray(np.concatenate([blocks(np.asarray(peer_wq)[0], 128), keys], 2)),
        "conv_w": np.ascontiguousarray(np.asarray(gdn_conv_w)[0].reshape(4, 12, 128).transpose(2, 1, 0)),
        "bias96": bias,
        "alog96": alog,
        "norm_w": np.asarray(gdn_norm_w)[0:1],
        "ln": np.ascontiguousarray(np.concatenate([ln1_g, ln1_b, ln2_g, ln2_b], 0)),
        "experts": np.ascontiguousarray(np.concatenate([np.asarray(peer_u)[0], np.asarray(peer_v)[0]], 1)),
    }
    nc = bacc.Bacc("TRN2", target_bir_lowering=False, num_devices=1)
    aps = {k: nc.dram_tensor("in_" + k, v.shape, mybir.dt.from_np(v.dtype), kind="ExternalInput").ap()
           for k, v in arrays.items()}
    out = nc.dram_tensor("out", (SEQ, D), F32, kind="ExternalOutput").ap()
    build(nc, out=out, **aps)
    r = run_bass_kernel_spmd(nc, [{"in_" + k: v for k, v in arrays.items()}], core_ids=[0])
    return r.results[0]["out"].reshape(1, SEQ, D)
```

```python
import concourse.bass as bass
from concourse import mybir
from contextlib import ExitStack

F32 = mybir.dt.float32
U32 = mybir.dt.uint32
ALU = mybir.AluOpType
ACT = mybir.ActivationFunctionType
AX = mybir.AxisListType

D = 1024
SEQ = 1024
P = 128
KB = D // P
T = 512
HALVES = SEQ // T
TT = T // P
GH = 4
FH = 8
FD = 64
PH = 8
TOPK = 16
ALPHA = 2.0 ** 0.25
NEG = -3.0e38
ROWS = 96
BETA0, FOX0 = 32, 64
LEVELS = 6
UNIT = 2
UNITS = TOPK // UNIT
GROUPS = TT * PH
ARENA = 19000

I_QKV, I_Z, I_SM, I_FQK, I_FV, I_MIX, I_WO, I_PQ = 0, 12, 13, 14, 22, 23, 31, 33
ITEMS = 49


def build(nc, x, xT, w_qkv, w_z, w_sm, w_fqk, w_fv, w_mix, w_out, w_pq, conv_w, bias96, alog96,
          norm_w, ln, experts, out):
    ctx = ExitStack()
    with ctx:
        def sb(name, shape, dt=F32):
            return ctx.enter_context(nc.sbuf_tensor(name, shape, dt))

        def sem(name):
            return ctx.enter_context(nc.semaphore(name))

        def sems(name, n=2):
            return [sem(f"{name}{i}") for i in range(n)]

        def dram(name, *shape):
            return nc.dram_tensor(name, list(shape), F32, kind="Internal").ap()

        B = [ctx.enter_context(nc.psum_tensor(f"bank{i}", [P, 512], F32)) for i in range(8)]
        BY = B[6:8]
        d_rows = dram("d_rows", ROWS, SEQ)
        d_qkv = dram("d_qkv", 12, P, SEQ)
        d_z = dram("d_z", SEQ, 512)
        d_fqk = dram("d_fqk", 8, P, SEQ)
        d_fv = dram("d_fv", SEQ, 512)
        d_h1 = dram("d_h1", SEQ, D)

        ident = sb("ident", [P, P])
        ones = sb("ones", [P, P])
        incl = sb("incl", [P, P])
        strict = sb("strict", [P, P])
        levmask = sb("levmask", [P, LEVELS + 1, P])
        negup = sb("negup", [P, P])
        state = sb("state", [P, GH, P])
        halo = sb("halo", [P, 12, 3])
        cw = sb("cw", [P, 12, 4])
        bias_c = sb("bias_c", [ROWS, 1])
        alog_c = sb("alog_c", [ROWS, 1])
        fcarry = sb("fcarry", [P, 1])
        eps_l2 = sb("eps_l2", [P, 1])
        normB = sb("normB", [P, P])
        ln2B = sb("ln2B", [P, 2, D])
        wslot = sb("wslot", [P, 2, 4096])
        eidx = sb("eidx", [P, HALVES, TT, PH, TOPK], U32)
        gate = sb("gate", [P, HALVES, TT, PH, TOPK])
        iota16 = sb("iota16", [P, TOPK])

        ringA = sb("ringA", [P, 8, 2 * D])
        h_cur, Y = sb("h_cur", [P, D]), sb("Y", [P, D])
        diag = sb("diag", [P, 2 * UNIT, P])
        dots, gel, gcur, wgt = (sb(n, [P, TOPK]) for n in ("dots", "gel", "gcur", "wgt"))
        istage, icur, izero, ispare = (
            sb(n, [P, w], U32) for n, w in (("istage", TOPK), ("icur", TOPK), ("izero", UNIT), ("ispare", UNIT)))
        pst, pmv = sb("pst", [P, 2, 6]), sb("pmv", [P, 2])

        arena = sb("arena", [P, ARENA])

        class Region:
            def __init__(self, at):
                self.at = at

            def take(self, *shape, rows=P):
                n = 1
                for s in shape:
                    n *= s
                v = arena[0:rows, self.at:self.at + n]
                self.at += n
                assert self.at <= ARENA, self.at
                if len(shape) == 2:
                    v = v.rearrange("p (a b) -> p a b", a=shape[0])
                if len(shape) == 3:
                    v = v.rearrange("p (a b c) -> p a b c", a=shape[0], b=shape[1])
                return v

        base = Region(0)
        oTg = base.take(GH, T)
        rowsT = base.take(TT, ROWS)
        r = Region(base.at)
        xTs = r.take(KB, T)
        raw = r.take(2, T + 3)
        acc = r.take(2, T)
        cwc = r.take(2, 4)
        fst = r.take(2, T)
        zs = r.take(TT, 512)
        fvs = r.take(TT, 512)
        sm = [r.take(T, rows=ROWS) for _ in range(6)]
        rows = r.take(T, rows=ROWS)
        onesr = r.take(T, rows=ROWS)
        r = Region(base.at)
        gB, bB = r.take(GH, P), r.take(GH, P)
        qkvt = r.take(12, P)
        zt = r.take(GH * P)
        sq = r.take(8, P)
        nr = r.take(8, P)
        qn, kn, kbT, qg, egB, DT, DTs, vt, kbg, kd, vb, MT, QK, X, Tm, Pm, wT, u, vn = (
            r.take(GH, P) for _ in range(19))
        MS = r.take(2, GH, P)
        o, og, osq = DTs, kbT, vt
        colS = r.take(ROWS)
        gd, egc, be, ss, rs4 = (r.take(GH) for _ in range(5))
        r = Region(GH * T)
        Osb = r.take(TT, 512)
        oTf = r.take(4, T)
        after_o = r.at
        qh = r.take(2, T, rows=FD)
        kh = r.take(2, SEQ, rows=FD)
        vh = r.take(2, SEQ // P, FD)
        cB = r.take(2, SEQ)
        cBd = r.take(TT, P)
        sx = r.take(2, SEQ)
        pT = r.take(SEQ // P, P)
        nm, rsum, rinv = r.take(2), r.take(2), r.take(2)
        r = Region(after_o)
        xTm = r.take(KB, T)
        mixT = r.take(KB, T)
        after_mix = r.at
        sg = r.take(2, 2, T)
        mt = r.take(2, T)
        r = Region(0)
        h1 = r.take(TT, D)
        after_h1 = r.at
        xn = r.take(TT, D)
        ln1B = r.take(2, D)
        assert r.at <= after_mix - KB * T
        r = Region(after_mix)
        h1T = r.take(KB, T)
        st, mv = r.take(2, 6), r.take(2)
        r = Region(after_h1)
        qp = r.take(2, T)
        sc = r.take(2, TT, P)
        tv, ti, tf = (r.take(2, TT, TOPK) for _ in range(3))
        cand = r.take(TT, 256)
        bv, bi, ba, bb, fa, fb = (r.take(TT, TOPK) for _ in range(6))
        eq = r.take(TT * TOPK, TOPK)
        gsum = r.take(TT)
        assert r.at <= after_mix
        ringB = Region(0).take(8, 2 * D)

        s_const, s_load, s_cst2 = sem("s_const"), sem("s_load"), sem("s_cst2")
        s_xT, s_xTm, s_xn = sem("s_xT"), sem("s_xTm"), sem("s_xn")
        s_w = sems("s_w")
        s_wdone = sem("s_wdone")
        s_raw, s_conv, s_silu = sems("s_raw"), sems("s_conv"), sems("s_silu")
        s_nat, s_natev = sem("s_nat"), sems("s_natev")
        s_smE, s_smU, s_smL, s_smX = sem("s_smE"), sem("s_smU"), sem("s_smL"), sem("s_smX")
        s_rows, s_rowst, s_rT, s_rTe = sem("s_rows"), sem("s_rowst"), sem("s_rT"), sem("s_rTe")
        s_gb, s_zst = sem("s_gb"), sem("s_zst")
        g = {k: sem("g_" + k) for k in (
            "sq", "ssum", "norm", "qk", "diff", "exps", "decay", "prod", "scaled", "kbg", "x0", "t0p",
            "t0", "ms", "lp", "lpe", "lt", "lx", "wu", "wte", "ws", "vn", "o", "S",
            "osq", "ss", "rt", "og", "ogt", "oT")}
        s_fev, s_fst, s_fvst = sems("s_fev"), sems("s_fst"), sem("s_fvst")
        s_att, s_attd = sems("s_att"), sems("s_attd")
        s_S, s_sc, s_ex = sems("s_S"), sems("s_sc"), sems("s_ex")
        s_T, s_Te, s_O, s_Oe = sem("s_T"), sem("s_Te"), sem("s_O"), sem("s_Oe")
        s_OT, s_OTe = sem("s_OT"), sem("s_OTe")
        s_ga, s_gb2, s_sga, s_sg, s_mix = sems("s_ga"), sems("s_gb2"), sems("s_sga"), sems("s_sg"), sems("s_mix")
        s_var, s_std, s_h1, s_h1st = sem("s_var"), sem("s_std"), sem("s_h1"), sem("s_h1st")
        s_hT, s_hTe = sem("s_hT"), sem("s_hTe")
        s_pq, s_pqe, s_scr, s_sce, s_top = sems("s_pq"), sems("s_pqe"), sems("s_scr"), sems("s_sce"), sems("s_top")
        s_gx, s_gxe, s_sel = sem("s_gx"), sem("s_gxe"), sem("s_sel")
        s_idx, s_stage, s_dot, s_gel, s_wgt, s_diag, s_yadd = (
            sem(n) for n in ("s_idx", "s_stage", "s_dot", "s_gel", "s_wgt", "s_diag", "s_yadd"))
        s_gat, s_pv = sems("s_gat", UNITS), sems("s_pv", UNITS)
        s_hc, s_yv, s_ys, s_y, s_out = sem("s_hc"), sem("s_yv"), sem("s_ys"), sem("s_y"), sem("s_out")

        block = ctx.enter_context(nc.Block())

        def item(n, w):
            return wslot[:, n % 2, 0:w * 128].rearrange("p (k c) -> p k c", k=w)

        def wide(n):
            return wslot[:, n % 2, :].rearrange("p (k c) -> p k c", k=KB)

        def flat(v):
            return v.rearrange("p a b -> p (a b)")

        def slots(hf, u):
            if hf == 0 or u < 4:
                return [ringA[:, UNIT * (u % 4) + k, :] for k in range(UNIT)]
            return [ringB[:, UNIT * (u - 4) + k, :] for k in range(UNIT)]

        def uses(hf, b, u):
            if hf == 0:
                return u % 4, 2 * b + u // 4
            return (u, b + 2 * GROUPS) if u < 4 else (u, b)

        @block.sync
        def _(sp):
            for dst, src, s in ((cw[:, :, :], conv_w, s_fst[0]), (bias_c[:, :], bias96, s_fst[1]),
                                (alog_c[:, :], alog96, s_out), (normB[:, :], norm_w.to_broadcast([P, P]), s_load)):
                sp.dma_start(dst, src).then_inc(s, 16)
            for k in range(2):
                sp.dma_start(ln2B[:, k, :], ln[2 + k:3 + k, :].to_broadcast([P, D])).then_inc(s_load, 16)

            def load(n, dst, src, i=0):
                if n >= 2:
                    sp.wait_ge(s_wdone, n - 1 + 2 * i)
                sp.dma_start(dst, src).then_inc(s_w[n % 2], 16)

            def load_pairs(first, w, src, at, count):
                with sp.Fori(0, count // 2) as i:
                    for j in range(2):
                        n = first + at + j
                        load(n, item(n, w), src[bass.ds(2 * i + (at + j), 1)].rearrange("a p k c -> p (a k) c"), i)

            for hf in range(HALVES):
                n0 = ITEMS * hf
                half = slice(hf * T, (hf + 1) * T)
                if hf:
                    sp.wait_ge(s_sel, PH * hf)
                    sp.wait_ge(s_h1st, 16 * hf)
                sp.dma_start(xTs, xT[:, half].rearrange("(k p) t -> p k t", p=P)).then_inc(s_xT, 16)
                for j in range(2):
                    load(n0 + j, item(n0 + j, 8), w_qkv[j])
                load_pairs(n0 + I_QKV, 8, w_qkv, 2, 10)
                load(n0 + I_Z, wide(n0 + I_Z), w_z)
                n = n0 + I_SM
                load(n, wslot[:, n % 2, 0:KB * ROWS].rearrange("p (k c) -> p k c", k=KB), w_sm)
                for j in range(2):
                    n = n0 + I_FQK + j
                    load(n, item(n, 8), w_fqk[j])
                sp.wait_ge(s_rows, hf + 1)
                sp.dma_start(d_rows[:, half], rows).then_inc(s_rowst, 16)
                load_pairs(n0 + I_FQK, 8, w_fqk, 2, 6)
                load(n0 + I_FV, wide(n0 + I_FV), w_fv)
                for j in range(2):
                    n = n0 + I_MIX + j
                    load(n, item(n, 24), w_mix[j])
                sp.wait_ge(s_rowst, 16 * (hf + 1))
                sp.wait_ge(s_zst, 16 * (hf + 1))
                sp.wait_ge(s_fvst, 16 * (hf + 1))
                for j in range(2):
                    sp.wait_ge(s_fst[j], 16 + 160 * (hf + 1))
                sp.wait_ge(s_rTe, hf + 1)
                with sp.Fori(0, TT) as c:
                    sp.wait_ge(g["og"], 1 + c + TT * hf)
                    for dst, r0 in ((gB, 0), (bB, BETA0)):
                        for h in range(GH):
                            sp.dma_start(dst[:, h, :], d_rows[r0 + h:r0 + h + 1, bass.ds(c * P + hf * T, P)]
                                         .to_broadcast([P, P])).then_inc(s_gb, 16)
                    sp.dma_start(qkvt, d_qkv[:, :, bass.ds(c * P + hf * T, P)].rearrange("a p t -> p a t")
                                 ).then_inc(s_gb, 16)
                    sp.dma_start(zt, d_z[bass.ds(c * P + hf * T, P), :]).then_inc(s_gb, 16)
                sp.wait_ge(g["oT"], 1 + TT * (hf + 1))
                W = T * (hf + 1)
                with sp.Fori(0, FH // 2) as i:
                    for j in range(2):
                        sp.wait_ge(s_attd[j], 1 + i + 4 * hf)
                        sp.dma_start(qh[:, j, :], d_fqk[bass.ds(2 * i, 1), FD * j:FD * (j + 1), half]
                                     .rearrange("a p t -> p (a t)")).then_inc(s_att[j], 16)
                        sp.dma_start(kh[:, j, 0:W], d_fqk[bass.ds(2 * i + 1, 1), FD * j:FD * (j + 1), 0:W]
                                     .rearrange("a p t -> p (a t)")).then_inc(s_att[j], 16)
                        sp.dma_start(vh[:, j, 0:W // P, :], d_fv[0:W, bass.ds(i * P + FD * j, FD)]
                                     .rearrange("(k p) d -> p k d", p=P)).then_inc(s_att[j], 16)
                        sp.dma_start(cB[:, j, 0:W], d_rows[bass.ds(2 * i + (FOX0 + j), 1), 0:W]
                                     .to_broadcast([P, W])).then_inc(s_att[j], 16)
                for j in range(2):
                    sp.wait_ge(s_attd[j], 1 + 4 * (hf + 1))
                sp.dma_start(xTm, xT[:, half].rearrange("(k p) t -> p k t", p=P)).then_inc(s_xTm, 16)
                load_pairs(n0 + I_MIX, 24, w_mix, 2, 6)
                for j in range(2):
                    load(n0 + I_WO + j, wide(n0 + I_WO + j), w_out[j])
                sp.wait_ge(s_wdone, n0 + I_WO)
                for j in range(2):
                    sp.wait_ge(s_mix[j], 1 + 4 * (hf + 1))
                sp.dma_start(xn, x[half, :].rearrange("(t p) d -> p t d", p=P)).then_inc(s_xn, 16)
                for k in range(2):
                    sp.dma_start(ln1B[:, k, :], ln[k:k + 1, :].to_broadcast([P, D])).then_inc(s_xn, 16)
                for j in range(2):
                    load(n0 + I_PQ + j, item(n0 + I_PQ + j, 9), w_pq[j])
                sp.wait_ge(s_h1, TT * (hf + 1))
                sp.dma_start(d_h1[half, :].rearrange("(t p) d -> p t d", p=P), h1).then_inc(s_h1st, 16)
                load_pairs(n0 + I_PQ, 9, w_pq, 2, 14)
            sp.wait_ge(s_out, 16 + 16 * TT * HALVES)

        @block.gpsimd
        def _(pool):
            for s in (*s_fev, *s_raw, *s_conv, *s_silu, *s_attd, *s_sc, s_T, s_O, s_Te, s_Oe, *s_mix, *s_pqe,
                      *s_sce, *s_top, *s_pv, s_yadd, g["lp"], g["S"], g["og"], g["oT"], s_diag, s_wgt):
                pool.sem_inc(s, 1)
            pool.memset(ones[:, :], 1.0)
            pool.memset(ident[:, :], 0.0)
            pool.memset(state[:, :, :], 0.0)
            pool.memset(halo[:, :, :], 0.0)
            pool.memset(fcarry[:, :], 0.0)
            pool.memset(eps_l2[:, :], 1e-6)
            pool.memset(negup[:, :], 1e30)
            pool.iota(iota16[:, :], [[1, TOPK]], base=0, channel_multiplier=0, allow_small_or_imprecise_dtypes=True)
            pool.drain()
            pool.affine_select(out=ident[:, :], in_=ident[:, :], compare_op=ALU.not_equal, fill=1.0, base=0,
                               pattern=[[-1, P]], channel_multiplier=1)
            pool.affine_select(out=incl[:, :], in_=ones[:, :], compare_op=ALU.is_ge, fill=0.0, base=0,
                               pattern=[[1, P]], channel_multiplier=-1)
            pool.affine_select(out=strict[:, :], in_=ones[:, :], compare_op=ALU.is_gt, fill=0.0, base=0,
                               pattern=[[1, P]], channel_multiplier=-1)
            pool.affine_select(out=negup[:, :], in_=negup[:, :], compare_op=ALU.is_gt, fill=0.0, base=0,
                               pattern=[[1, P]], channel_multiplier=-1)
            for l in range(LEVELS + 1):
                s = 1 << l
                nb = P // (2 * s)
                v = levmask[:, l, :].rearrange("p (b h r) -> p b h r", b=nb, h=2)
                pool.memset(v[:, :, 0, :], 0.0)
                w = v[:, :, 1, :]
                pool.drain()
                pool.affine_select(out=w, in_=ones[:, 0:nb * s].rearrange("p (b r) -> p b r", b=nb),
                                   compare_op=ALU.is_ge, fill=0.0, base=0,
                                   pattern=[[-2 * s, nb], [0, s]], channel_multiplier=1)
                pool.drain()
                pool.affine_select(out=w, in_=w, compare_op=ALU.is_gt, fill=0.0, base=s,
                                   pattern=[[2 * s, nb], [0, s]], channel_multiplier=-1)
            pool.drain()
            pool.memset(izero[:, :], 0).then_inc(s_const, 1)
            n_idx = [0]

            for hf in range(HALVES):
                def stage(b):
                    pool.tensor_copy(istage[:, :], eidx[:, hf, :, :, :].rearrange("p t h k -> p (t h) k")
                                     [:, bass.ds(b, 1), :].rearrange("p a k -> p (a k)")).then_inc(s_stage, 1)

                def gates(b):
                    pool.tensor_copy(gcur[:, :], gate[:, hf, :, :, :].rearrange("p t h k -> p (t h) k")
                                     [:, bass.ds(b, 1), :].rearrange("p a k -> p (a k)")).then_inc(s_stage, 1)

                def gather(b, u):
                    k = slice(UNIT * u, UNIT * (u + 1))
                    r, used = uses(hf, b, u)
                    pool.wait_ge(s_pv[r], used + 1)
                    pool.tensor_tensor(icur[:, k], istage[:, k], izero[:, :], ALU.add).then_inc(s_idx, 1)
                    pool.wait_ge(s_idx, 2 * UNITS * b + (2 * UNITS * GROUPS * hf + 2 * u + 1))
                    pool.tensor_tensor(ispare[:, :], izero[:, :], izero[:, :], ALU.add).then_inc(s_idx, 1)
                    for n, slot in enumerate(slots(hf, u)):
                        c = UNIT * u + n
                        pool.indirect_dma_start(
                            out=slot, out_offset=None, in_=experts,
                            in_offset=bass.IndirectOffsetOnAxis(ap=icur[:, c:c + 1], axis=0),
                        ).then_inc(s_gat[r], 16)

                def weigh(b, u):
                    k = slice(UNIT * u, UNIT * (u + 1))
                    pool.wait_ge(s_gel, UNITS * b + (UNITS * GROUPS * hf + u + 1))
                    pool.tensor_tensor(wgt[:, k], gel[:, k], gcur[:, k], ALU.mult).then_inc(s_wgt, 1)

                ahead = 4 if hf == 0 else UNITS
                pool.wait_ge(s_sel, PH * (hf + 1))
                if hf:
                    pool.wait_ge(s_h1st, 16 * (hf + 1))
                    pool.wait_ge(s_wdone, ITEMS * HALVES)
                pool.wait_ge(s_idx, 2 * UNITS * GROUPS * hf) if hf else None
                stage(0)
                pool.wait_ge(s_stage, 2 * GROUPS * hf + 1)
                for u in range(ahead):
                    gather(0, u)

                def group(b, more):
                    pool.wait_ge(s_wgt, UNITS * b + (UNITS * GROUPS * hf + 1))
                    gates(b)
                    for u in range(UNITS):
                        if u + ahead == UNITS and more:
                            pool.wait_ge(s_idx, 2 * UNITS * b + 2 * UNITS * (GROUPS * hf + 1))
                            stage(b + 1)
                            pool.wait_ge(s_stage, 2 * b + (2 * GROUPS * hf + 3))
                        elif u == 0:
                            pool.wait_ge(s_stage, 2 * b + (2 * GROUPS * hf + 2))
                        if u == 0:
                            weigh(b, 0)
                        if u + 1 < UNITS:
                            weigh(b, u + 1)
                        v = u + ahead
                        if v < UNITS:
                            gather(b, v)
                        elif more:
                            gather(b + 1, v - UNITS)

                with pool.Fori(0, GROUPS - 1) as b:
                    group(b, True)
                group(GROUPS - 1, False)

        @block.scalar
        def _(act):
            act.wait_ge(s_const, 1)
            act.wait_ge(s_load, 16 * 3)
            act.wait_ge(s_fst[0], 16)
            act.wait_ge(s_fst[1], 16)
            act.wait_ge(s_out, 16)
            act.activation(alog_c[:, :], alog_c[:, :], ACT.Exp).then_inc(s_cst2, 1)

            def peer(hf, b, u0, u1):
                for u in range(u0, u1):
                    k = slice(UNIT * u, UNIT * (u + 1))
                    n = UNITS * b + (UNITS * GROUPS * hf + u + 1)
                    act.wait_ge(s_dot, n)
                    act.activation(gel[:, k], dots[:, k], ACT.Gelu).then_inc(s_gel, 1)
                    act.wait_ge(s_wgt, n + 1)
                    if u >= 2:
                        r, used = uses(hf, b, u - 2)
                        act.wait_ge(s_pv[r], used + 2)
                    for c in range(UNIT * u, UNIT * (u + 1)):
                        last = act.activation(diag[:, c % (2 * UNIT), :], ident[:, :], ACT.Copy, scale=wgt[:, c:c + 1])
                    last.then_inc(s_diag, 1)

            def group_end(hf, b):
                for u in (UNITS - 2, UNITS - 1):
                    r, used = uses(hf, b, u)
                    act.wait_ge(s_pv[r], used + 2)

            def load_h(tile):
                act.dma_start(h_cur[:, :], d_h1[bass.ds(tile * P, P), :]).then_inc(s_hc, 16)

            def tile_end(tile, more=True):
                act.wait_ge(s_yv, tile + 1)
                act.activation(pmv[:, 1:2], pmv[:, 1:2], ACT.Sqrt).then_inc(s_ys, 1)
                act.wait_ge(s_y, tile + 1)
                act.dma_start(out[bass.ds(tile * P, P), :], Y[:, :]).then_inc(s_out, 16)
                if more:
                    load_h(tile + 1)

            def store_block(j, n_blk, dst):
                act.dma_start(dst, fst[:, j, :]).then_inc(s_fst[j], 16)

            for hf in range(HALVES):
                on = hf > 0
                n0 = ITEMS * hf
                half = slice(hf * T, (hf + 1) * T)
                if on:
                    act.wait_ge(s_h1st, 16)
                    load_h(0)
                with act.Fori(0, 3) as i:
                    for j in range(4):
                        r, c = j % 2, 2 * i + (j // 2 + 6 * hf)
                        act.wait_ge(s_wdone, 4 * i + (n0 + j + 1))
                        act.wait_ge(s_conv[r], 1 + c)
                        act.activation(raw[:, r, 3:T + 3], B[r][:, :], ACT.Copy).then_inc(s_raw[r], 1)
                        act.wait_ge(s_conv[r], 2 + c)
                        act.wait_ge(s_fst[r], 32 * i + (16 + 160 * hf + 16 * (j // 2)))
                        act.activation(fst[:, r, :], acc[:, r, :], ACT.Silu).then_inc(s_silu[r], 1)
                        act.wait_ge(s_silu[r], 2 + c)
                        act.dma_start(d_qkv[bass.ds(4 * i + j, 1), :, half].rearrange("a p t -> p (a t)"),
                                      fst[:, r, :]).then_inc(s_fst[r], 16)
                        if on:
                            peer(0, i, 2 * j, 2 * j + 2)
                    if on:
                        group_end(0, i)
                for tt in range(TT):
                    act.wait_ge(s_nat, 16 * hf + tt + 1)
                    act.activation(zs[:, tt, :], B[2 + tt % 2][:, :], ACT.Silu).then_inc(s_natev[tt % 2], 1)
                    if on:
                        peer(0, 3, tt, tt + 1)
                for k in range(2):
                    act.wait_ge(s_natev[k], 8 * hf + 2)
                act.dma_start(d_z[half, :].rearrange("(t p) c -> p t c", p=P), zs).then_inc(s_zst, 16)
                act.wait_ge(s_smE, hf + 1)
                act.activation(sm[2], sm[1], ACT.Exp, scale=-1.0)
                act.activation(sm[5], sm[0], ACT.Exp, scale=-1.0).then_inc(s_smX, 1)
                act.wait_ge(s_smU, hf + 1)
                act.activation(sm[4], sm[3], ACT.Ln).then_inc(s_smL, 1)
                act.wait_ge(s_rT, hf + 1)
                act.activation(rowsT[:, :, :], B[5][:, 0:TT * ROWS].rearrange("p (a b) -> p a b", a=TT),
                               ACT.Copy).then_inc(s_rTe, 1)
                if on:
                    peer(0, 3, 4, 8)
                    group_end(0, 3)
                with act.Fori(0, 2) as i:
                    for j in range(4):
                        r = j % 2
                        act.wait_ge(s_wdone, 4 * i + (n0 + I_FQK + j + 1))
                        act.wait_ge(s_fst[r], 32 * i + (16 + 160 * hf + 96 + 16 * (j // 2)))
                        act.activation(fst[:, r, :], B[r][:, :], ACT.Copy,
                                       scale=(FD ** -0.5 if r == 0 else 1.0)).then_inc(s_fev[r], 1)
                        act.wait_ge(s_fev[r], 2 * i + (2 + j // 2 + 4 * hf))
                        act.dma_start(d_fqk[bass.ds(4 * i + j, 1), :, half].rearrange("a p t -> p (a t)"),
                                      fst[:, r, :]).then_inc(s_fst[r], 16)
                        if on:
                            peer(0, 4 + i, 2 * j, 2 * j + 2)
                    if on:
                        group_end(0, 4 + i)
                for tt in range(TT):
                    act.wait_ge(s_nat, 16 * hf + 4 + tt + 1)
                    act.activation(fvs[:, tt, :], B[2 + tt % 2][:, :], ACT.Copy).then_inc(s_natev[tt % 2], 1)
                    if on:
                        peer(0, 6, 2 * tt, 2 * tt + 2)
                for k in range(2):
                    act.wait_ge(s_natev[k], 8 * hf + 4)
                act.dma_start(d_fv[half, :].rearrange("(t p) c -> p t c", p=P), fvs).then_inc(s_fvst, 16)
                if on:
                    group_end(0, 6)
                    peer(0, 7, 0, 8)
                    tile_end(0)
                with act.Fori(0, TT) as c:
                    tau = c + (TT * hf + 1)
                    act.wait_ge(g["ssum"], tau)
                    for k in range(2):
                        act.activation(flat(nr[:, 4 * k:4 * k + 4, :]), B[k][:, :],
                                       ACT.Sqrt, bias=eps_l2[:, :]).then_inc(g["norm"], 1)
                    act.wait_ge(g["diff"], tau)
                    act.activation(egB, gB, ACT.Exp)
                    act.activation(DT, DT, ACT.Exp)
                    act.activation(gd, gd, ACT.Exp)
                    act.activation(egc, colS[:, 0:GH], ACT.Exp)
                    act.activation(vt, qkvt[:, 8:12, :], ACT.Copy).then_inc(g["exps"], 1)
                    if on:
                        peer(0, 8 + 2 * c, 0, 2)
                    act.wait_ge(g["prod"], tau)
                    for h in range(GH):
                        act.activation(kd[:, h, :], B[2][:, h * P:(h + 1) * P], ACT.Copy, scale=gd[:, h:h + 1])
                        last = act.activation(vb[:, h, :], B[3][:, h * P:(h + 1) * P], ACT.Copy,
                                              scale=colS[:, BETA0 + h:BETA0 + h + 1])
                    last.then_inc(g["scaled"], 1)
                    act.wait_ge(g["t0p"], tau)
                    act.activation(flat(Tm), B[1][:, :], ACT.Copy).then_inc(g["t0"], 1)
                    for l in range(LEVELS):
                        act.wait_ge(g["lp"], c * LEVELS + (TT * hf * LEVELS + l + 2))
                        act.activation(flat(Pm), B[4][:, :], ACT.Copy).then_inc(g["lpe"], 1)
                        if on:
                            peer(0, 8 + 2 * c, l + 2, l + 3)
                    if on:
                        group_end(0, 8 + 2 * c)
                    act.wait_ge(g["wu"], tau)
                    act.activation(flat(wT), B[1][:, :], ACT.Copy).then_inc(g["wte"], 1)
                    if on:
                        peer(0, 9 + 2 * c, 0, 3)
                    act.wait_ge(g["o"], tau)
                    act.activation(flat(o), B[4][:, :], ACT.Copy)
                    act.drain()
                    act.activation(osq, o, ACT.Square).then_inc(g["osq"], 1)
                    if on:
                        peer(0, 9 + 2 * c, 3, 6)
                    act.wait_ge(g["ss"], tau)
                    act.activation(rs4, ss, ACT.Sqrt).then_inc(g["rt"], 1)
                    act.wait_ge(g["ogt"], tau)
                    act.activation(oTg[:, :, bass.ds(c * P, P)],
                                   B[0][:, :].rearrange("p (a b) -> p a b", a=GH), ACT.Copy).then_inc(g["oT"], 1)
                    if on:
                        peer(0, 9 + 2 * c, 6, 8)
                        group_end(0, 9 + 2 * c)
                if on:
                    tile_end(1)
                with act.Fori(0, FH // 2) as i:
                    it = i + 4 * hf

                    def softmax(m):
                        nk = 4 * hf + m % 4 + 1
                        act.wait_ge(s_sc[m % 2], 4 * it + (m // 2 + 2))
                        act.activation(sx[:, m % 2, 0:nk * P], sx[:, m % 2, 0:nk * P], ACT.Exp,
                                       bias=nm[:, m % 2:m % 2 + 1],
                                       accum_out=rsum[:, m % 2:m % 2 + 1]).then_inc(s_ex[m % 2], 1)

                    softmax(0)
                    for m in range(8):
                        if m < 7:
                            softmax(m + 1)
                        nk = 4 * hf + m % 4 + 1
                        act.wait_ge(s_T, 8 * it + (m + 2))
                        act.wait_ge(s_O, 8 * it + (m + 1))
                        for k0 in range(0, nk, 4):
                            k1 = min(nk, k0 + 4)
                            last = act.activation(flat(pT[:, k0:k1, :]), B[4 + k0 // 4][:, 0:(k1 - k0) * P], ACT.Copy)
                        last.then_inc(s_Te, 1)
                        if on:
                            peer(0, 16 + i, m, m + 1)
                    if on:
                        group_end(0, 16 + i)
                for tt in range(TT):
                    act.wait_ge(s_OT, 4 * hf + tt + 1)
                    act.activation(oTf[:, :, tt * P:(tt + 1) * P],
                                   B[4 + tt % 2][:, :].rearrange("p (a b) -> p a b", a=4), ACT.Copy).then_inc(s_OTe, 1)
                with act.Fori(0, 4) as i:
                    for j in range(2):
                        it = i + (4 * hf + 1)
                        act.wait_ge(s_ga[j], it)
                        act.wait_ge(s_mix[j], it)
                        act.activation(sg[:, j, 0, :], B[3 * j][:, :], ACT.Sigmoid).then_inc(s_sga[j], 1)
                        act.wait_ge(s_gb2[j], it)
                        act.activation(sg[:, j, 1, :], B[3 * j + 2][:, :], ACT.Sigmoid).then_inc(s_sg[j], 1)
                        if on:
                            peer(0, 20 + i, *((0, 2), (2, 8))[j])
                    if on:
                        group_end(0, 20 + i)
                if on:
                    tile_end(2)
                for tt in range(TT):
                    act.wait_ge(s_var, 4 * hf + tt + 1)
                    act.activation(mv[:, 1:2], mv[:, 1:2], ACT.Sqrt).then_inc(s_std, 1)
                for tt in range(TT):
                    act.wait_ge(s_hT, 4 * hf + tt + 1)
                    for k in range(2):
                        last = act.activation(h1T[:, 4 * k:4 * k + 4, tt * P:(tt + 1) * P],
                                              B[2 * (tt % 2) + k][:, :].rearrange("p (a b) -> p a b", a=4), ACT.Copy)
                    last.then_inc(s_hTe, 1)
                with act.Fori(0, PH) as i:
                    it = i + (PH * hf + 1)
                    for j in range(2):
                        act.wait_ge(s_pq[j], it)
                        act.activation(qp[:, j, :], B[j][:, :], ACT.Copy).then_inc(s_pqe[j], 1)
                    for j in range(2):
                        act.wait_ge(s_scr[j], it)
                        act.wait_ge(s_top[j], it)
                        act.activation(sc[:, j, :, :], B[2 + j][:, :].rearrange("p (a b) -> p a b", a=TT),
                                       ACT.Copy).then_inc(s_sce[j], 1)
                        if on:
                            peer(0, 24 + i, 2 * j, 2 * j + 2)
                    act.wait_ge(s_gx, it)
                    act.activation(bv, bv, ACT.Exp).then_inc(s_gxe, 1)
                    if on:
                        peer(0, 24 + i, 4, 8)
                        group_end(0, 24 + i)
                if on:
                    tile_end(3, more=False)
            act.wait_ge(s_h1st, 32)
            with act.Fori(0, TT) as t:
                load_h(t + TT)
                with act.Fori(0, PH) as h:
                    peer(1, t * PH + h, 0, UNITS)
                    group_end(1, t * PH + h)
                act.wait_ge(s_yv, t + (TT + 1))
                act.activation(pmv[:, 1:2], pmv[:, 1:2], ACT.Sqrt).then_inc(s_ys, 1)
                act.wait_ge(s_y, t + (TT + 1))
                act.dma_start(out[bass.ds(t * P + T, P), :], Y[:, :]).then_inc(s_out, 16)

        @block.vector
        def _(dve):
            dve.wait_ge(s_const, 1)
            dve.wait_ge(s_load, 16 * 3)
            dve.wait_ge(s_fst[0], 16)
            dve.wait_ge(s_fst[1], 16)
            dve.wait_ge(s_out, 16)
            dve.wait_ge(s_cst2, 1)
            dve.tensor_scalar(alog_c[:, :], alog_c[:, :], -1.0, None, ALU.mult)
            dve.drain()

            def top16(vals, v16, i16):
                dve.max(v16[:, 0:8], vals)
                dve.drain()
                dve.max_index(i16[:, 0:8].bitcast(U32), v16[:, 0:8], vals)
                dve.drain()
                dve.match_replace(vals, v16[:, 0:8], vals, NEG)
                dve.drain()
                dve.max(v16[:, 8:16], vals)
                dve.drain()
                dve.max_index(i16[:, 8:16].bitcast(U32), v16[:, 8:16], vals)

            def layernorm(v, gb, stats, mean_var, s_v, s_s, s_val):
                for k in range(2):
                    dve.bn_stats(stats[:, k, :], v[:, k * 512:(k + 1) * 512])
                dve.drain()
                dve.bn_aggr(mean_var[:, 0:2], flat(stats[:, :, :]))
                dve.drain()
                dve.tensor_scalar(mean_var[:, 1:2], mean_var[:, 1:2], 1e-5, None, ALU.add).then_inc(s_v, 1)
                dve.wait_ge(s_s, s_val)
                dve.reciprocal(mean_var[:, 1:2], mean_var[:, 1:2])
                dve.drain()
                dve.tensor_scalar(v, v, mean_var[:, 0:1], mean_var[:, 1:2], ALU.subtract, ALU.mult)
                dve.drain()
                dve.tensor_tensor(v, v, gb[:, 0, :], ALU.mult)
                dve.drain()
                return dve.tensor_tensor(v, v, gb[:, 1, :], ALU.add)

            def peer(hf, b, u0, u1):
                for u in range(u0, u1):
                    r, used = uses(hf, b, u)
                    dve.wait_ge(s_gat[r], 16 * UNIT * used + 16 * UNIT)
                    for n, slot in enumerate(slots(hf, u)):
                        c = UNIT * u + n
                        last = dve.tensor_tensor_reduce(
                            out=slot[:, 0:D], in0=slot[:, 0:D], in1=h_cur[:, :], scale=1.0, scalar=0.0,
                            op0=ALU.mult, op1=ALU.add, accum_out=dots[:, c:c + 1])
                    last.then_inc(s_dot, 1)

            def group_end(hf, b):
                dve.drain()
                r, used = uses(hf, b, UNITS - 1)
                dve.wait_ge(s_pv[r], used + 2)
                for k in range(2):
                    last = dve.tensor_tensor(Y[:, k * 512:(k + 1) * 512], Y[:, k * 512:(k + 1) * 512],
                                             BY[k][:, :], ALU.add)
                last.then_inc(s_yadd, 1)

            def tile_start(tile):
                dve.wait_ge(s_hc, 16 * tile + 16)
                dve.wait_ge(s_out, 16 * tile + 16)
                dve.tensor_scalar(Y[:, :], h_cur[:, :], ALPHA, None, ALU.mult)

            def tile_end(tile):
                dve.drain()
                layernorm(Y[:, :], ln2B, pst, pmv, s_yv, s_ys, tile + 1).then_inc(s_y, 1)

            for hf in range(HALVES):
                on = hf > 0
                n0 = ITEMS * hf
                if on:
                    tile_start(0)
                with dve.Fori(0, 3) as i:
                    for j in range(4):
                        r, c = j % 2, 2 * i + (j // 2 + 6 * hf)
                        rj, aj = raw[:, r, :], acc[:, r, :]
                        blk = bass.ds(4 * i + j, 1)
                        dve.wait_ge(s_silu[r], 1 + c)
                        dve.tensor_copy(cwc[:, r, :], flat(cw[:, blk, :]))
                        dve.tensor_copy(rj[:, 0:3], flat(halo[:, blk, :]))
                        dve.drain()
                        dve.wait_ge(s_raw[r], 2 + c)
                        dve.tensor_scalar(aj, rj[:, 0:T], cwc[:, r, 0:1], None, ALU.mult)
                        for k in range(1, 4):
                            dve.drain()
                            last = dve.scalar_tensor_tensor(aj, rj[:, k:k + T], cwc[:, r, k:k + 1], aj,
                                                            ALU.mult, ALU.add)
                            if k == 1:
                                dve.tensor_copy(flat(halo[:, blk, :]), rj[:, T:T + 3])
                        last.then_inc(s_conv[r], 1)
                        if on:
                            peer(0, i, 2 * j, 2 * j + 2)
                    if on:
                        group_end(0, i)
                if on:
                    peer(0, 3, 0, 4)
                dve.wait_ge(s_wdone, n0 + I_SM + 1)
                V, A, E, U, L, XS = sm
                dve.tensor_scalar(V, B[4][0:ROWS, :], bias_c[:, :], None, ALU.add)
                dve.memset(onesr, 1.0)
                dve.drain()
                dve.scalar_tensor_tensor(A, V, -1.0, V, ALU.mult, ALU.max).then_inc(s_smE, 1)
                dve.wait_ge(s_smX, hf + 1)
                dve.tensor_scalar(U, E, 1.0, None, ALU.add).then_inc(s_smU, 1)
                dve.drain()
                dve.tensor_scalar(A, U, -1.0, None, ALU.add)
                dve.drain()
                dve.tensor_scalar(rows, A, 0.0, None, ALU.is_equal)
                dve.drain()
                dve.tensor_scalar(A, A, 1e-30, None, ALU.max)
                dve.tensor_tensor(rows, rows, E, ALU.mult)
                dve.drain()
                dve.reciprocal(A, A)
                dve.drain()
                dve.tensor_tensor(A, A, E, ALU.mult)
                dve.drain()
                dve.wait_ge(s_smL, hf + 1)
                dve.tensor_tensor(L, L, A, ALU.mult)
                dve.drain()
                dve.tensor_tensor(L, L, rows, ALU.add)
                dve.tensor_scalar(A, V, 0.0, None, ALU.max)
                dve.tensor_scalar(U, V, 0.0, None, ALU.min)
                dve.tensor_scalar(XS, XS, 1.0, None, ALU.add)
                dve.drain()
                dve.tensor_tensor(A, A, L, ALU.add)
                dve.tensor_tensor(U, U, L, ALU.subtract)
                dve.reciprocal(rows, XS)
                dve.drain()
                dve.tensor_scalar(A, A, alog_c[:, :], None, ALU.mult)
                dve.drain()
                for tt in range(TT):
                    s = slice(tt * P, (tt + 1) * P)
                    dve.tensor_tensor_scan(rows[0:GH, s], onesr[0:GH, s], A[0:GH, s], 0.0, ALU.mult, ALU.add)
                dve.tensor_tensor_scan(rows[FOX0:FOX0 + FH, :], onesr[FOX0:FOX0 + FH, :], U[FOX0:FOX0 + FH, :],
                                       fcarry[FOX0:FOX0 + FH, :], ALU.mult, ALU.add).then_inc(s_rows, 1)
                dve.drain()
                dve.tensor_copy(fcarry[FOX0:FOX0 + FH, :], rows[FOX0:FOX0 + FH, T - 1:T])
                if on:
                    peer(0, 3, 4, 8)
                    group_end(0, 3)
                    with dve.Fori(0, 2) as i:
                        peer(0, 4 + i, 0, 8)
                        group_end(0, 4 + i)
                    peer(0, 6, 0, 8)
                    group_end(0, 6)
                    peer(0, 7, 0, 8)
                    group_end(0, 7)
                    tile_end(0)
                    tile_start(1)
                dve.wait_ge(s_rTe, hf + 1)
                dve.wait_ge(s_rowst, 16 * (hf + 1))
                dve.wait_ge(s_zst, 16 * (hf + 1))
                dve.wait_ge(s_fvst, 16 * (hf + 1))
                for j in range(2):
                    dve.wait_ge(s_fst[j], 16 + 160 * (hf + 1))
                with dve.Fori(0, TT) as c:
                    tau = c + (TT * hf + 1)
                    dve.drain()
                    dve.wait_ge(s_gb, 160 * c + 160 * (TT * hf + 1))
                    dve.tensor_tensor(sq, qkvt[:, 0:8, :], qkvt[:, 0:8, :], ALU.mult).then_inc(g["sq"], 1)
                    dve.tensor_copy(colS, flat(rowsT[:, bass.ds(c, 1), :]))
                    dve.drain()
                    for h in range(GH):
                        dve.tensor_scalar(DT[:, h, :], gB[:, h, :], colS[:, h:h + 1], 0.0, ALU.subtract, ALU.min)
                    dve.tensor_tensor(gd, gB[:, :, P - 1], colS[:, 0:GH], ALU.subtract).then_inc(g["diff"], 1)
                    dve.wait_ge(g["norm"], 2 * c + 2 * (TT * hf + 1))
                    dve.reciprocal(nr, nr)
                    dve.drain()
                    dve.scalar_tensor_tensor(qn, qkvt[:, 0:4, :], P ** -0.5, nr[:, 0:4, :], ALU.mult, ALU.mult)
                    dve.tensor_tensor(kn, qkvt[:, 4:8, :], nr[:, 4:8, :], ALU.mult)
                    dve.drain()
                    dve.tensor_tensor(kbT, kn, bB, ALU.mult).then_inc(g["qk"], 1)
                    dve.wait_ge(g["exps"], tau)
                    dve.tensor_tensor(DT, DT, incl[:, None, :].to_broadcast([P, GH, P]), ALU.mult)
                    dve.tensor_tensor(qg, qn, egB, ALU.mult)
                    dve.tensor_tensor(be, egc, colS[:, BETA0:BETA0 + GH], ALU.mult)
                    dve.drain()
                    dve.tensor_tensor(DTs, DT, strict[:, None, :].to_broadcast([P, GH, P]), ALU.mult)
                    if on:
                        peer(0, 8 + 2 * c, 0, 2)
                    dve.drain()
                    dve.wait_ge(g["prod"], tau)
                    dve.tensor_tensor(flat(MT), B[4][:, :], flat(DTs), ALU.mult)
                    dve.drain()
                    dve.tensor_tensor(X, MT, levmask[:, 0:1, :].to_broadcast([P, GH, P]), ALU.mult)
                    dve.drain()
                    dve.tensor_tensor(X, ident[:, None, :].to_broadcast([P, GH, P]), X, ALU.subtract).then_inc(g["x0"], 1)
                    for l in range(2):
                        dve.tensor_tensor(MS[:, l, :, :], MT, levmask[:, l + 1:l + 2, :].to_broadcast([P, GH, P]),
                                          ALU.mult).then_inc(g["ms"], 1)
                    dve.tensor_tensor(flat(QK), B[5][:, :], flat(DT), ALU.mult)
                    dve.wait_ge(g["scaled"], tau)
                    for h in range(GH):
                        last = dve.tensor_scalar(kbg[:, h, :], B[2][:, h * P:(h + 1) * P], be[:, h:h + 1], None, ALU.mult)
                    last.then_inc(g["kbg"], 1)
                    dve.drain()
                    dve.wait_ge(g["t0"], tau)
                    for l in range(LEVELS):
                        if l:
                            dve.drain()
                        dve.wait_ge(g["lt"], c * LEVELS + (TT * hf * LEVELS + l + 1))
                        if l < LEVELS - 1:
                            dve.tensor_tensor(flat(Tm), flat(Tm), B[1][:, :], ALU.subtract)
                        dve.tensor_tensor(flat(X), flat(X), B[0][:, :], ALU.subtract).then_inc(g["lx"], 1)
                        if l + 2 < LEVELS:
                            dve.tensor_tensor(MS[:, l % 2, :, :], MT, levmask[:, l + 3:l + 4, :].to_broadcast([P, GH, P]),
                                              ALU.mult).then_inc(g["ms"], 1)
                        if on:
                            peer(0, 8 + 2 * c, l + 2, l + 3)
                    if on:
                        group_end(0, 8 + 2 * c)
                    dve.wait_ge(g["wu"], tau)
                    dve.tensor_copy(flat(u), B[2][:, :])
                    dve.drain()
                    dve.wait_ge(g["ws"], tau)
                    dve.tensor_tensor(flat(vn), flat(u), B[3][:, :], ALU.subtract).then_inc(g["vn"], 1)
                    if on:
                        peer(0, 9 + 2 * c, 0, 3)
                    dve.wait_ge(g["o"], tau)
                    for h in range(GH):
                        last = dve.scalar_tensor_tensor(state[:, h, :], state[:, h, :], egB[:, h, P - 1:P],
                                                        B[5][:, h * P:(h + 1) * P], ALU.mult, ALU.add)
                    last.then_inc(g["S"], 1)
                    if on:
                        peer(0, 9 + 2 * c, 3, 6)
                    dve.wait_ge(g["osq"], tau)
                    dve.tensor_reduce(ss, osq, AX.X, ALU.add)
                    dve.drain()
                    dve.tensor_scalar(ss, ss, 1.0 / P, 1e-6, ALU.mult, ALU.add).then_inc(g["ss"], 1)
                    dve.wait_ge(g["rt"], tau)
                    dve.reciprocal(rs4, rs4)
                    dve.drain()
                    for h in range(GH):
                        dve.scalar_tensor_tensor(og[:, h, :], o[:, h, :], rs4[:, h:h + 1], normB[:, :], ALU.mult, ALU.mult)
                    dve.drain()
                    dve.tensor_tensor(flat(og), flat(og), zt, ALU.mult).then_inc(g["og"], 1)
                    if on:
                        peer(0, 9 + 2 * c, 6, 8)
                        group_end(0, 9 + 2 * c)
                if on:
                    tile_end(1)
                    tile_start(2)
                dve.wait_ge(g["oT"], 1 + TT * (hf + 1))
                with dve.Fori(0, FH // 2) as i:
                    it = i + 4 * hf

                    def scores(m):
                        j, qt, r = m // 4, m % 4, m % 2
                        nk = 4 * hf + qt + 1
                        if qt == 0:
                            dve.wait_ge(s_att[j], 64 * it + 64)
                            dve.tensor_tensor(cBd, cB[:, j, hf * T:(hf + 1) * T].rearrange("p (a b) -> p a b", a=TT),
                                              negup[:, None, :].to_broadcast([P, TT, P]), ALU.add)
                            dve.drain()
                        dve.wait_ge(s_S[r], 4 * it + (m // 2 + 1))
                        dve.wait_ge(s_T, 8 * it + max(m, 1))
                        n_full = (nk - 1) * P
                        for k0 in range(0, n_full, 512):
                            k1 = min(n_full, k0 + 512)
                            dve.tensor_tensor(sx[:, r, k0:k1], B[2 * r + k0 // 512][:, 0:k1 - k0], cB[:, j, k0:k1],
                                              ALU.subtract)
                        off = n_full % 512
                        dve.tensor_tensor(sx[:, r, n_full:n_full + P], B[2 * r + n_full // 512][:, off:off + P],
                                          cBd[:, qt, :], ALU.subtract)
                        dve.drain()
                        dve.tensor_reduce(nm[:, r:r + 1], sx[:, r, 0:nk * P], AX.X, ALU.max, negate=True).then_inc(s_sc[r], 1)

                    scores(0)
                    for m in range(8):
                        if m < 7:
                            scores(m + 1)
                        j, qt, r = m // 4, m % 4, m % 2
                        dve.wait_ge(s_O, 8 * it + (m + 2))
                        dve.reciprocal(rinv[:, r:r + 1], rsum[:, r:r + 1])
                        dve.drain()
                        dve.tensor_scalar(Osb[:, qt, bass.ds(i * P + FD * j, FD)], B[4][:, 0:FD], rinv[:, r:r + 1],
                                          None, ALU.mult).then_inc(s_Oe, 1)
                        if qt == 3:
                            dve.drain().then_inc(s_attd[j], 1)
                        if on:
                            peer(0, 16 + i, m, m + 1)
                    if on:
                        group_end(0, 16 + i)
                with dve.Fori(0, 4) as i:
                    for j in range(2):
                        dve.drain()
                        dve.wait_ge(s_sg[j], i + (4 * hf + 1))
                        dve.wait_ge(s_wdone, 2 * i + (n0 + I_MIX + j + 1))
                        for k in range(2):
                            dve.tensor_tensor(mt[:, k, :], sg[:, j, k, :], B[3 * j + 1 - k][:, :], ALU.mult)
                        dve.drain()
                        dve.tensor_tensor(flat(mixT[:, bass.ds(2 * i + j, 1), :]), mt[:, 0, :], mt[:, 1, :],
                                          ALU.add).then_inc(s_mix[j], 1)
                        if on:
                            peer(0, 20 + i, 4 * j, 4 * j + 4)
                    if on:
                        group_end(0, 20 + i)
                if on:
                    tile_end(2)
                    tile_start(3)
                dve.wait_ge(s_xn, 48 * (hf + 1))
                for nh in range(2):
                    for tt in range(TT):
                        dve.wait_ge(s_nat, 16 * hf + 8 + 4 * nh + tt + 1)
                        dve.scalar_tensor_tensor(h1[:, tt, nh * 512:(nh + 1) * 512], xn[:, tt, nh * 512:(nh + 1) * 512],
                                                 ALPHA, B[2 + tt % 2][:, :], ALU.mult, ALU.add).then_inc(s_natev[tt % 2], 1)
                dve.drain()
                for tt in range(TT):
                    layernorm(h1[:, tt, :], ln1B, st, mv, s_var, s_std, 4 * hf + tt + 1).then_inc(s_h1, 1)
                    dve.drain()
                with dve.Fori(0, PH) as i:
                    for j in range(2):
                        dve.wait_ge(s_sce[j], i + (PH * hf + 2))
                        dve.memset(tv[:, j, :, :], NEG)
                        dve.drain()
                        for tt in range(TT):
                            top16(sc[:, j, tt, :], tv[:, j, tt, :], ti[:, j, tt, :])
                        dve.drain()
                        dve.tensor_copy(tf[:, j, :, :], ti[:, j, :, :].bitcast(U32)).then_inc(s_top[j], 1)
                        if on:
                            peer(0, 24 + i, 2 * j, 2 * j + 2)
                    dve.drain()
                    for tt in range(TT):
                        dve.tensor_tensor(cand[:, tt, :].rearrange("p (a b) -> p a b", a=TOPK),
                                          tv[:, 0, tt, :, None].to_broadcast([P, TOPK, TOPK]),
                                          tv[:, 1, tt, None, :].to_broadcast([P, TOPK, TOPK]), ALU.add)
                    dve.drain()
                    for tt in range(TT):
                        top16(cand[:, tt, :], bv[:, tt, :], bi[:, tt, :])
                    dve.drain()
                    dve.tensor_scalar(ba.bitcast(U32), bi.bitcast(U32), 4, None, ALU.logical_shift_right)
                    dve.tensor_scalar(bb.bitcast(U32), bi.bitcast(U32), 15, None, ALU.bitwise_and)
                    for tt in range(TT):
                        dve.tensor_scalar(gsum[:, tt:tt + 1], bv[:, tt, 0:1], 1.0, None, ALU.mult)
                    dve.drain()
                    for tt in range(TT):
                        last = dve.tensor_scalar(bv[:, tt, :], bv[:, tt, :], gsum[:, tt:tt + 1], None, ALU.subtract)
                    last.then_inc(s_gx, 1)
                    if on:
                        peer(0, 24 + i, 4, 6)
                    for src, f, k in ((ba, fa, 0), (bb, fb, 1)):
                        dve.tensor_copy(f, src.bitcast(U32))
                        dve.drain()
                        dve.tensor_tensor(eq, flat(f)[:, :, None].to_broadcast([P, TT * TOPK, TOPK]),
                                          iota16[:, None, :].to_broadcast([P, TT * TOPK, TOPK]), ALU.is_equal)
                        dve.drain()
                        for tt in range(TT):
                            e = eq[:, tt * TOPK:(tt + 1) * TOPK, :]
                            dve.tensor_tensor(e, e, tf[:, k, tt, None, :].to_broadcast([P, TOPK, TOPK]), ALU.mult)
                        dve.drain()
                        dve.tensor_reduce(flat(f), eq, AX.X, ALU.add)
                        dve.drain()
                    dve.scalar_tensor_tensor(eidx[:, hf, :, bass.ds(i, 1), :].rearrange("p t a k -> p t (a k)"),
                                             fa, float(P), fb, ALU.mult, ALU.add)
                    dve.wait_ge(s_gxe, i + (PH * hf + 1))
                    dve.tensor_reduce(gsum, bv, AX.X, ALU.add)
                    dve.drain()
                    dve.reciprocal(gsum, gsum)
                    dve.drain()
                    dve.tensor_tensor(gate[:, hf, :, bass.ds(i, 1), :].rearrange("p t a k -> p t (a k)"), bv,
                                      gsum[:, :, None].to_broadcast([P, TT, TOPK]), ALU.mult).then_inc(s_sel, 1)
                    dve.drain()
                    if on:
                        peer(0, 24 + i, 6, 8)
                        group_end(0, 24 + i)
                if on:
                    tile_end(3)
            with dve.Fori(0, TT) as t:
                tile_start(t + TT)
                with dve.Fori(0, PH) as h:
                    peer(1, t * PH + h, 0, UNITS)
                    group_end(1, t * PH + h)
                tile_end(t + TT)

        @block.tensor
        def _(pe):
            pe.wait_ge(s_const, 1)

            def peer(hf, b, u0, u1):
                for u in range(u0, u1):
                    if u == 0:
                        pe.wait_ge(s_yadd, b + (GROUPS * hf + 1))
                    pe.wait_ge(s_diag, UNITS * b + (UNITS * GROUPS * hf + u + 2))
                    r, used = uses(hf, b, u)
                    for m, slot in enumerate(slots(hf, u)):
                        c = UNIT * u + m
                        for n in range(2):
                            last = pe.matmul(BY[n][:, :], diag[:, c % (2 * UNIT), :],
                                             slot[:, D + n * 512:D + (n + 1) * 512],
                                             start=(c == 0), stop=(c == TOPK - 1))
                    last.then_inc(s_pv[r], 1)

            def block_mm(bank, w, rhs, nk=KB, k0=0):
                for k in range(nk):
                    last = pe.matmul(bank[:, :], w[:, k0 + k, :], rhs[:, k, :], start=(k == 0), stop=(k == nk - 1))
                return last

            def natural(n, call, hf, lhs, between=None):
                pe.wait_ge(s_w[n % 2], 16 * (n // 2 + 1))
                w = wide(n)
                for tt in range(TT):
                    pe.wait_ge(s_natev[tt % 2], 8 * hf + 2 * call + tt // 2)
                    for k in range(KB):
                        last = pe.matmul(B[2 + tt % 2][:, :], lhs[:, k, tt * P:(tt + 1) * P], w[:, k, :],
                                         start=(k == 0), stop=(k == KB - 1))
                    last.then_inc(s_nat, 1)
                    if between:
                        between(tt)
                pe.drain().then_inc(s_wdone, 1)

            def transpose4(bank, src):
                for h in range(4):
                    last = pe.transpose(bank[:, h * P:(h + 1) * P], src[:, h, :], ident[:, :])
                return last

            def heads(bank, lhs, rhs):
                for h in range(GH):
                    last = pe.matmul(bank[:, h * P:(h + 1) * P], lhs[:, h, :], rhs[:, h, :], start=True, stop=True)
                return last

            for hf in range(HALVES):
                on = hf > 0
                n0 = ITEMS * hf
                pe.wait_ge(s_xT, 16 * (hf + 1))
                with pe.Fori(0, 3) as i:
                    for j in range(4):
                        n = n0 + j
                        pe.wait_ge(s_w[n % 2], 32 * i + 16 * (n // 2 + 1))
                        pe.wait_ge(s_raw[j % 2], 2 * i + (1 + j // 2 + 6 * hf))
                        block_mm(B[j % 2], item(n, 8), xTs).then_inc(s_wdone, 1)
                        if on and j:
                            peer(0, i, 2 * j - 2, 2 * j)
                    if on:
                        peer(0, i, 6, 8)
                natural(n0 + I_Z, 0, hf, xTs, (lambda tt: peer(0, 3, tt - 1, tt) if tt else None) if on else None)
                n = n0 + I_SM
                pe.wait_ge(s_w[n % 2], 16 * (n // 2 + 1))
                w = wslot[:, n % 2, 0:KB * ROWS].rearrange("p (k c) -> p k c", k=KB)
                for k in range(KB):
                    last = pe.matmul(B[4][0:ROWS, :], w[:, k, :], xTs[:, k, :], start=(k == 0), stop=(k == KB - 1))
                last.then_inc(s_wdone, 1)
                if on:
                    peer(0, 3, 3, 4)
                pe.wait_ge(s_rows, hf + 1)
                for tt in range(TT):
                    last = pe.transpose(B[5][:, tt * ROWS:(tt + 1) * ROWS], rows[:, tt * P:(tt + 1) * P],
                                        ident[0:ROWS, 0:ROWS])
                last.then_inc(s_rT, 1)
                if on:
                    peer(0, 3, 4, 8)
                pe.wait_ge(s_raw[0], 1 + 6 * (hf + 1))
                pe.wait_ge(s_raw[1], 1 + 6 * (hf + 1))
                with pe.Fori(0, 2) as i:
                    for j in range(4):
                        n = n0 + I_FQK + j
                        pe.wait_ge(s_w[n % 2], 32 * i + 16 * (n // 2 + 1))
                        pe.wait_ge(s_fev[j % 2], 2 * i + (1 + j // 2 + 4 * hf))
                        block_mm(B[j % 2], item(n, 8), xTs).then_inc(s_wdone, 1)
                        if on and j:
                            peer(0, 4 + i, 2 * j - 2, 2 * j)
                    if on:
                        peer(0, 4 + i, 6, 8)
                natural(n0 + I_FV, 1, hf, xTs, (lambda tt: peer(0, 6, 2 * tt - 2, 2 * tt) if tt else None) if on else None)
                for k in range(2):
                    pe.wait_ge(s_natev[k], 8 * hf + 4)
                    pe.wait_ge(s_fev[k], 1 + 4 * (hf + 1))
                if on:
                    peer(0, 6, 6, 8)
                    peer(0, 7, 0, 8)
                with pe.Fori(0, TT) as c:
                    tau = c + (TT * hf + 1)
                    lev = c * LEVELS
                    pe.wait_ge(g["sq"], tau)
                    pe.wait_ge(g["oT"], tau)
                    for k in range(2):
                        last = pe.matmul(B[k][:, :], ones[:, :], flat(sq[:, 4 * k:4 * k + 4, :]), start=True, stop=True)
                    last.then_inc(g["ssum"], 1)
                    pe.wait_ge(g["qk"], tau)
                    pe.wait_ge(g["exps"], tau)
                    transpose4(B[2], kn)
                    transpose4(B[3], vt)
                    heads(B[4], kn, kbT)
                    heads(B[5], kn, qn).then_inc(g["prod"], 1)
                    if on:
                        peer(0, 8 + 2 * c, 0, 2)
                    pe.wait_ge(g["x0"], tau)
                    transpose4(B[1], X).then_inc(g["t0p"], 1)
                    pe.wait_ge(g["t0"], tau)
                    for l in range(LEVELS):
                        pe.wait_ge(g["ms"], lev + (TT * hf * LEVELS + l + 1))
                        if l:
                            pe.wait_ge(g["lx"], lev + (TT * hf * LEVELS + l))
                        heads(B[4], MS[:, l % 2, :, :], Tm).then_inc(g["lp"], 1)
                        if on and l:
                            peer(0, 8 + 2 * c, l + 1, l + 2)
                        pe.wait_ge(g["lpe"], lev + (TT * hf * LEVELS + l + 1))
                        if l < LEVELS - 1:
                            heads(B[1], X, Pm)
                        heads(B[0], Pm, X).then_inc(g["lt"], 1)
                    if on:
                        peer(0, 8 + 2 * c, 7, 8)
                    pe.wait_ge(g["lx"], lev + (TT * hf * LEVELS + LEVELS))
                    pe.wait_ge(g["kbg"], tau)
                    heads(B[1], kbg, X)
                    heads(B[2], X, vb).then_inc(g["wu"], 1)
                    pe.wait_ge(g["wte"], tau)
                    pe.wait_ge(g["S"], c + (TT * hf + 1))
                    heads(B[3], wT, state).then_inc(g["ws"], 1)
                    pe.wait_ge(g["vn"], tau)
                    for h in range(GH):
                        s = slice(h * P, (h + 1) * P)
                        pe.matmul(B[4][:, s], qg[:, h, :], state[:, h, :], start=True, stop=False)
                        pe.matmul(B[4][:, s], QK[:, h, :], vn[:, h, :], start=False, stop=True)
                    heads(B[5], kd, vn).then_inc(g["o"], 1)
                    if on:
                        peer(0, 9 + 2 * c, 0, 6)
                    pe.wait_ge(g["og"], tau + 1)
                    transpose4(B[0], og).then_inc(g["ogt"], 1)
                    if on:
                        peer(0, 9 + 2 * c, 6, 8)
                pe.wait_ge(g["oT"], 1 + TT * (hf + 1))
                with pe.Fori(0, FH // 2) as i:
                    it = i + 4 * hf

                    def qk_scores(m):
                        j, qt, r = m // 4, m % 4, m % 2
                        nk = 4 * hf + qt + 1
                        if qt == 0:
                            pe.wait_ge(s_att[j], 64 * it + 64)
                        pe.wait_ge(s_sc[r], 4 * it + (m // 2 + 1))
                        for k0 in range(0, nk * P, 512):
                            k1 = min(nk * P, k0 + 512)
                            last = pe.matmul(B[2 * r + k0 // 512][:, 0:k1 - k0], qh[:, j, qt * P:(qt + 1) * P],
                                             kh[:, j, k0:k1], start=True, stop=True)
                        last.then_inc(s_S[r], 1)

                    qk_scores(0)
                    for m in range(8):
                        if m < 7:
                            qk_scores(m + 1)
                        j, qt, r = m // 4, m % 4, m % 2
                        nk = 4 * hf + qt + 1
                        pe.wait_ge(s_ex[r], 4 * it + (m // 2 + 1))
                        pe.wait_ge(s_Te, 8 * it + (m + 1))
                        pe.wait_ge(s_Oe, 8 * it + (m + 1))
                        for k in range(nk):
                            last = pe.transpose(B[4 + k // 4][:, (k % 4) * P:(k % 4 + 1) * P],
                                                sx[:, r, k * P:(k + 1) * P], ident[:, :])
                        last.then_inc(s_T, 1)
                        if on and m:
                            peer(0, 16 + i, m - 1, m)
                        pe.wait_ge(s_Te, 8 * it + (m + 2))
                        for k in range(nk):
                            last = pe.matmul(B[4][:, 0:FD], pT[:, k, :], vh[:, j, k, :], start=(k == 0), stop=(k == nk - 1))
                        last.then_inc(s_O, 1)
                    if on:
                        peer(0, 16 + i, 7, 8)
                pe.wait_ge(s_Oe, 1 + 32 * (hf + 1))
                for tt in range(TT):
                    if tt >= 2:
                        pe.wait_ge(s_OTe, 4 * hf + tt - 1)
                    transpose4(B[4 + tt % 2], Osb[:, tt, :].rearrange("p (a b) -> p a b", a=4)).then_inc(s_OT, 1)
                pe.wait_ge(s_OTe, 4 * (hf + 1))
                pe.wait_ge(s_xTm, 16 * (hf + 1))
                with pe.Fori(0, 4) as i:
                    for j in range(2):
                        n = n0 + I_MIX + j
                        it = i + (4 * hf + 1)
                        pe.wait_ge(s_w[n % 2], 16 * i + 16 * (n // 2 + 1))
                        pe.wait_ge(s_mix[j], it)
                        w = item(n, 24)
                        block_mm(B[3 * j], w, xTm).then_inc(s_ga[j], 1)
                        block_mm(B[3 * j + 1], w, oTg, nk=4, k0=16)
                        block_mm(B[3 * j + 2], w, xTm, k0=8).then_inc(s_gb2[j], 1)
                        if on and j:
                            peer(0, 20 + i, 0, 2)
                        pe.wait_ge(s_sga[j], it)
                        block_mm(B[3 * j], w, oTf, nk=4, k0=20).then_inc(s_wdone, 1)
                    if on:
                        peer(0, 20 + i, 2, 8)
                for j in range(2):
                    pe.wait_ge(s_mix[j], 1 + 4 * (hf + 1))
                for nh in range(2):
                    natural(n0 + I_WO + nh, 2 + nh, hf, mixT)
                for k in range(2):
                    pe.wait_ge(s_natev[k], 8 * (hf + 1))
                for tt in range(TT):
                    pe.wait_ge(s_h1, 4 * hf + tt + 1)
                    if tt >= 2:
                        pe.wait_ge(s_hTe, 4 * hf + tt - 1)
                    for k in range(2):
                        last = transpose4(B[2 * (tt % 2) + k],
                                          h1[:, tt, k * 512:(k + 1) * 512].rearrange("p (a b) -> p a b", a=4))
                    last.then_inc(s_hT, 1)
                pe.wait_ge(s_hTe, 4 * (hf + 1))
                with pe.Fori(0, PH) as i:
                    for j in range(2):
                        n = n0 + I_PQ + j
                        pe.wait_ge(s_w[n % 2], 16 * i + 16 * (n // 2 + 1))
                        pe.wait_ge(s_pqe[j], i + (PH * hf + 1))
                        block_mm(B[j], item(n, 9), h1T).then_inc(s_pq[j], 1)
                    for j in range(2):
                        n = n0 + I_PQ + j
                        pe.wait_ge(s_pqe[j], i + (PH * hf + 2))
                        pe.wait_ge(s_sce[j], i + (PH * hf + 1))
                        for tt in range(TT):
                            last = pe.matmul(B[2 + j][:, tt * P:(tt + 1) * P], qp[:, j, tt * P:(tt + 1) * P],
                                             item(n, 9)[:, 8, :], start=True, stop=True)
                        last.then_inc(s_scr[j], 1)
                    pe.drain().then_inc(s_wdone, 2)
                    if on:
                        peer(0, 24 + i, 0, 8)
            with pe.Fori(0, TT) as t:
                with pe.Fori(0, PH) as h:
                    peer(1, t * PH + h, 0, UNITS)


def kernel(x, w_in, gdn_conv_w, gdn_a_log, gdn_dt_bias, gdn_norm_w, fox_f_bias, w_out_gdn, w_out_fox,
           w_o, ln1_g, ln1_b, peer_wq, peer_keys, peer_u, peer_v, ln2_g, ln2_b):
    import numpy as np
    import concourse.bacc as bacc
    from concourse.bass_utils import run_bass_kernel_spmd

    def blocks(w, width):
        k, n = w.shape
        return np.ascontiguousarray(w.reshape(k // 128, 128, n // width, width).transpose(2, 1, 0, 3))

    w = np.asarray(w_in)[0]
    o = np.cumsum([0, 512, 512, 512, 512, 4, 4, 512, 512, 512, 8, 1024, 1024])
    small = np.zeros((1024, ROWS), np.float32)
    small[:, 0:4], small[:, BETA0:BETA0 + 4], small[:, FOX0:FOX0 + 8] = (
        w[:, o[4]:o[5]], w[:, o[5]:o[6]], w[:, o[9]:o[10]])
    fq, fk = blocks(w[:, o[6]:o[7]], 128), blocks(w[:, o[7]:o[8]], 128)
    bias = np.zeros((ROWS, 1), np.float32)
    bias[0:4, 0], bias[FOX0:FOX0 + 8, 0] = gdn_dt_bias[0], fox_f_bias[0]
    alog = np.zeros((ROWS, 1), np.float32)
    alog[0:4, 0] = gdn_a_log[0]
    keys = np.asarray(peer_keys)[0].reshape(16, 128, 128).transpose(0, 2, 1)[:, :, None, :]
    arrays = {
        "x": np.asarray(x)[0],
        "xT": np.ascontiguousarray(np.asarray(x)[0].T),
        "w_qkv": blocks(w[:, 0:o[3]], 128),
        "w_z": blocks(w[:, o[3]:o[4]], 512)[0],
        "w_sm": blocks(small, ROWS)[0],
        "w_fqk": np.ascontiguousarray(np.stack([fq, fk], 1).reshape(8, 128, 8, 128)),
        "w_fv": blocks(w[:, o[8]:o[9]], 512)[0],
        "w_mix": np.ascontiguousarray(np.concatenate(
            [blocks(w[:, o[10]:o[11]], 128), blocks(w[:, o[11]:o[12]], 128),
             blocks(np.asarray(w_out_gdn)[0], 128), blocks(np.asarray(w_out_fox)[0], 128)], 2)),
        "w_out": blocks(np.asarray(w_o)[0], 512),
        "w_pq": np.ascontiguousarray(np.concatenate([blocks(np.asarray(peer_wq)[0], 128), keys], 2)),
        "conv_w": np.ascontiguousarray(np.asarray(gdn_conv_w)[0].reshape(4, 12, 128).transpose(2, 1, 0)),
        "bias96": bias,
        "alog96": alog,
        "norm_w": np.asarray(gdn_norm_w)[0:1],
        "ln": np.ascontiguousarray(np.concatenate([ln1_g, ln1_b, ln2_g, ln2_b], 0)),
        "experts": np.ascontiguousarray(np.concatenate([np.asarray(peer_u)[0], np.asarray(peer_v)[0]], 1)),
    }
    nc = bacc.Bacc("TRN2", target_bir_lowering=False, num_devices=1)
    aps = {k: nc.dram_tensor("in_" + k, v.shape, mybir.dt.from_np(v.dtype), kind="ExternalInput").ap()
           for k, v in arrays.items()}
    out = nc.dram_tensor("out", (SEQ, D), F32, kind="ExternalOutput").ap()
    build(nc, out=out, **aps)
    r = run_bass_kernel_spmd(nc, [{"in_" + k: v for k, v in arrays.items()}], core_ids=[0])
    return r.results[0]["out"].reshape(1, SEQ, D)
```
